# Optimizing a Trainium2 kernel written in Bass

```python
import math
import jax
import jax.numpy as jnp
from jax import lax
import numpy as np

D_MODEL = 1024
BATCH = 1
SEQ = 256
DEPTH = 1

HEAD_DIM = 64
DIFF_WIDTH = D_MODEL // 2
DIFF_V_DIM = 2 * HEAD_DIM
N_DIFF_HEADS = DIFF_WIDTH // DIFF_V_DIM
MOBA_WIDTH = D_MODEL - DIFF_WIDTH
N_MOBA_HEADS = MOBA_WIDTH // HEAD_DIM
MIX_WIDTH = DIFF_WIDTH + MOBA_WIDTH
DQ_COLS = N_DIFF_HEADS * 2 * HEAD_DIM
DK_COLS = N_DIFF_HEADS * 2 * HEAD_DIM
DV_COLS = N_DIFF_HEADS * DIFF_V_DIM
MQ_COLS = N_MOBA_HEADS * HEAD_DIM
MK_COLS = N_MOBA_HEADS * HEAD_DIM
MV_COLS = N_MOBA_HEADS * HEAD_DIM
IN_WIDTH = DQ_COLS + DK_COLS + DV_COLS + MQ_COLS + MK_COLS + MV_COLS

Q_BLOCK = 128
MOBA_Q_BLOCK = 64
MOBA_BLOCK = 256
MOBA_TOPK = 3

N_BUCKETS = 32
MAX_DISTANCE = 128
N_BIAS_HEADS = N_DIFF_HEADS + N_MOBA_HEADS

N_GROUPS = 4
EXPERTS_PER_GROUP = 8
N_EXPERTS = N_GROUPS * EXPERTS_PER_GROUP
EXPERT_TOPK = 2
EXPERT_FF = D_MODEL // 2

EPS = 1e-6
NEG = -1e30

kernel_name = "hymba_diff_moba_hmoe_block"

def rmsnorm(x, gain):
    xf = x.astype(jnp.float32)
    y = xf * lax.rsqrt(jnp.mean(xf * xf, axis=-1, keepdims=True) + EPS)
    return (y * gain.astype(jnp.float32)).astype(x.dtype)

def rel_bucket(dist):
    n = jnp.maximum(dist, 0)
    max_exact = N_BUCKETS // 2
    nf = jnp.maximum(n, 1).astype(jnp.float32)
    large = max_exact + (jnp.log(nf / max_exact) / math.log(MAX_DISTANCE / max_exact)
                         * (N_BUCKETS - max_exact)).astype(jnp.int32)
    large = jnp.minimum(large, N_BUCKETS - 1)
    return jnp.where(n < max_exact, n, large)

def diff_attention(q, k, v, lam, bias_table):
    b, h, _, s, dh = q.shape
    nqb = s // Q_BLOCK
    qb = q.reshape(b, h, 2, nqb, Q_BLOCK, dh).transpose(3, 0, 1, 2, 4, 5)
    k_pos = jnp.arange(s)
    scale = dh ** -0.5

    def block(args):
        qi, i = args
        q_pos = i * Q_BLOCK + jnp.arange(Q_BLOCK)
        dist = q_pos[:, None] - k_pos[None, :]
        bias = jnp.moveaxis(bias_table[rel_bucket(dist)], -1, 0).astype(jnp.float32)
        sc = jnp.einsum('bhmqd,bhmkd->bhmqk', qi, k).astype(jnp.float32) * scale
        sc = sc + bias[None, :, None]
        sc = jnp.where(dist >= 0, sc, NEG)
        p = jax.nn.softmax(sc, axis=-1)
        a = p[:, :, 0] - lam * p[:, :, 1]
        return jnp.einsum('bhqk,bhkd->bhqd', a.astype(v.dtype), v)

    out = lax.map(block, (qb, jnp.arange(nqb)))
    return out.transpose(1, 2, 0, 3, 4).reshape(b, h, s, v.shape[-1])

def moba_attention(q, k, v, bias_table):
    b, h, s, dh = q.shape
    nkb = -(-s // MOBA_BLOCK)
    s_pad = nkb * MOBA_BLOCK
    pad = ((0, 0), (0, 0), (0, s_pad - s), (0, 0))
    k_p = jnp.pad(k, pad)
    v_p = jnp.pad(v, pad)
    kb = k_p.reshape(b, h, nkb, MOBA_BLOCK, dh)
    vb = v_p.reshape(b, h, nkb, MOBA_BLOCK, dh)
    k_mean = jnp.mean(kb.astype(jnp.float32), axis=3)
    topk = min(MOBA_TOPK, nkb)
    nqb = s // MOBA_Q_BLOCK
    qb = q.reshape(b, h, nqb, MOBA_Q_BLOCK, dh).transpose(2, 0, 1, 3, 4)
    blk_pos = jnp.arange(MOBA_BLOCK)
    tab_t = bias_table.T.astype(jnp.float32)
    h_idx = jnp.arange(h)[None, :, None, None, None]
    scale = dh ** -0.5
    gather = jax.vmap(jax.vmap(lambda blocks, idx: blocks[idx]))

    def block(args):
        qi, i = args
        q_pos = i * MOBA_Q_BLOCK + jnp.arange(MOBA_Q_BLOCK)
        own = (i * MOBA_Q_BLOCK) // MOBA_BLOCK
        g = jnp.einsum('bhqd,bhnd->bhqn', qi.astype(jnp.float32), k_mean)
        g = jnp.where(jnp.arange(nkb) < own, g, -jnp.inf)
        _, sel = lax.top_k(g, topk)
        valid = sel < own
        ks = gather(kb, sel)
        vs = gather(vb, sel)
        kpos_sel = sel[..., None] * MOBA_BLOCK + blk_pos
        dist_sel = q_pos[None, None, :, None, None] - kpos_sel
        s_sel = jnp.einsum('bhqd,bhqjkd->bhqjk', qi, ks).astype(jnp.float32) * scale
        s_sel = s_sel + tab_t[h_idx, rel_bucket(dist_sel)]
        s_sel = jnp.where(valid[..., None], s_sel, NEG)
        k_own = lax.dynamic_slice_in_dim(k_p, own * MOBA_BLOCK, MOBA_BLOCK, axis=2)
        v_own = lax.dynamic_slice_in_dim(v_p, own * MOBA_BLOCK, MOBA_BLOCK, axis=2)
        dist_own = q_pos[:, None] - (own * MOBA_BLOCK + blk_pos)[None, :]
        bias_own = jnp.moveaxis(bias_table[rel_bucket(dist_own)], -1, 0).astype(jnp.float32)
        s_own = jnp.einsum('bhqd,bhkd->bhqk', qi, k_own).astype(jnp.float32) * scale
        s_own = jnp.where(dist_own >= 0, s_own + bias_own[None], NEG)
        n_sel = topk * MOBA_BLOCK
        sc = jnp.concatenate([s_sel.reshape(b, h, MOBA_Q_BLOCK, n_sel), s_own], axis=-1)
        p = jax.nn.softmax(sc, axis=-1).astype(v.dtype)
        p_sel = p[..., :n_sel].reshape(b, h, MOBA_Q_BLOCK, topk, MOBA_BLOCK)
        p_own = p[..., n_sel:]
        return (jnp.einsum('bhqjk,bhqjkd->bhqd', p_sel, vs)
                + jnp.einsum('bhqk,bhkd->bhqd', p_own, v_own))

    out = lax.map(block, (qb, jnp.arange(nqb)))
    return out.transpose(1, 2, 0, 3, 4).reshape(b, h, s, dh)

def token_mixer(h, w_in, lq1, lk1, lq2, lk2, head_gain, w_out, rel_bias, lambda_init):
    b, s, _ = h.shape
    proj = h @ w_in
    splits = np.cumsum([DQ_COLS, DK_COLS, DV_COLS, MQ_COLS, MK_COLS]).tolist()
    dq, dk, dv, mq, mk, mv = jnp.split(proj, splits, axis=-1)
    dq = dq.reshape(b, s, N_DIFF_HEADS, 2, HEAD_DIM).transpose(0, 2, 3, 1, 4)
    dk = dk.reshape(b, s, N_DIFF_HEADS, 2, HEAD_DIM).transpose(0, 2, 3, 1, 4)
    dv = dv.reshape(b, s, N_DIFF_HEADS, DIFF_V_DIM).transpose(0, 2, 1, 3)
    mq = mq.reshape(b, s, N_MOBA_HEADS, HEAD_DIM).transpose(0, 2, 1, 3)
    mk = mk.reshape(b, s, N_MOBA_HEADS, HEAD_DIM).transpose(0, 2, 1, 3)
    mv = mv.reshape(b, s, N_MOBA_HEADS, HEAD_DIM).transpose(0, 2, 1, 3)

    lam = (jnp.exp(jnp.sum(lq1.astype(jnp.float32) * lk1.astype(jnp.float32)))
           - jnp.exp(jnp.sum(lq2.astype(jnp.float32) * lk2.astype(jnp.float32)))
           + lambda_init)
    y_diff = diff_attention(dq, dk, dv, lam, rel_bias[:, :N_DIFF_HEADS])
    y_diff = rmsnorm(y_diff, head_gain) * (1.0 - lambda_init)
    y_moba = moba_attention(mq, mk, mv, rel_bias[:, N_DIFF_HEADS:])

    y = jnp.concatenate([y_diff.transpose(0, 2, 1, 3).reshape(b, s, DIFF_WIDTH),
                         y_moba.transpose(0, 2, 1, 3).reshape(b, s, MOBA_WIDTH)], axis=-1)
    return y @ w_out

def hier_moe(h, w_group, b_group, w_expert, b_expert, w_gate, w_up, w_down):
    n = h.shape[0]
    rows = jnp.arange(n)
    gl = (h @ w_group + b_group).astype(jnp.float32)
    gp = jax.nn.softmax(gl, axis=-1)
    g_idx = jnp.argmax(gl, axis=-1)
    g_w = gp[rows, g_idx]
    el = (h @ w_expert + b_expert).astype(jnp.float32).reshape(n, N_GROUPS, EXPERTS_PER_GROUP)
    ep = jax.nn.softmax(el[rows, g_idx], axis=-1)
    tv, ti = lax.top_k(ep, EXPERT_TOPK)
    tv = tv / jnp.sum(tv, axis=-1, keepdims=True)
    wts = g_w[:, None] * tv
    e_idx = g_idx[:, None] * EXPERTS_PER_GROUP + ti
    gates = jnp.sum(jax.nn.one_hot(e_idx, N_EXPERTS, dtype=jnp.float32) * wts[..., None], axis=1)
    gates = gates.astype(h.dtype)

    def expert(acc, prm):
        wg, wu, wd, gt = prm
        hid = jax.nn.silu(h @ wg) * (h @ wu)
        return acc + gt[:, None] * (hid @ wd), None

    out, _ = lax.scan(expert, jnp.zeros_like(h), (w_gate, w_up, w_down, gates.T))
    return out

def setup_inputs(seed: int = 0) -> dict:
    key = jax.random.key(seed)
    ks = jax.random.split(key, 24)
    f32 = jnp.float32
    nrm = lambda k, shape, s: jax.random.normal(k, shape, f32) * s
    gain = lambda k, shape: 1.0 + 0.05 * jax.random.normal(k, shape, f32)
    d = D_MODEL
    return {
        "x": nrm(ks[0], (BATCH, SEQ, d), 1.0),
        "c": nrm(ks[1], (BATCH, d), 1.0),
        "w_ada": nrm(ks[2], (DEPTH, d, 6 * d), 0.5 * d ** -0.5),
        "b_ada": nrm(ks[3], (DEPTH, 6 * d), 0.01),
        "pre_mix_gain": gain(ks[4], (DEPTH, d)),
        "post_mix_gain": gain(ks[5], (DEPTH, d)),
        "pre_ffn_gain": gain(ks[6], (DEPTH, d)),
        "post_ffn_gain": gain(ks[7], (DEPTH, d)),
        "w_in": nrm(ks[8], (DEPTH, d, IN_WIDTH), d ** -0.5),
        "lambda_q1": nrm(ks[9], (DEPTH, HEAD_DIM), 0.1),
        "lambda_k1": nrm(ks[10], (DEPTH, HEAD_DIM), 0.1),
        "lambda_q2": nrm(ks[11], (DEPTH, HEAD_DIM), 0.1),
        "lambda_k2": nrm(ks[12], (DEPTH, HEAD_DIM), 0.1),
        "diff_head_gain": gain(ks[13], (DEPTH, DIFF_V_DIM)),
        "w_out": nrm(ks[14], (DEPTH, MIX_WIDTH, d), MIX_WIDTH ** -0.5),
        "rel_bias": nrm(ks[15], (N_BUCKETS, N_BIAS_HEADS), 0.5),
        "w_group": nrm(ks[16], (DEPTH, d, N_GROUPS), d ** -0.5),
        "b_group": nrm(ks[17], (DEPTH, N_GROUPS), 0.01),
        "w_expert": nrm(ks[18], (DEPTH, d, N_EXPERTS), d ** -0.5),
        "b_expert": nrm(ks[19], (DEPTH, N_EXPERTS), 0.01),
        "w_gate": nrm(ks[20], (DEPTH, N_EXPERTS, d, EXPERT_FF), d ** -0.5),
        "w_up": nrm(ks[21], (DEPTH, N_EXPERTS, d, EXPERT_FF), d ** -0.5),
        "w_down": nrm(ks[22], (DEPTH, N_EXPERTS, EXPERT_FF, d), EXPERT_FF ** -0.5),
    }

def reference(x, c, w_ada, b_ada, pre_mix_gain, post_mix_gain, pre_ffn_gain, post_ffn_gain,
              w_in, lambda_q1, lambda_k1, lambda_q2, lambda_k2, diff_head_gain, w_out,
              rel_bias, w_group, b_group, w_expert, b_expert, w_gate, w_up, w_down):
    b, s, d = x.shape
    for l in range(DEPTH):
        lambda_init = 0.8 - 0.6 * math.exp(-0.3 * l)
        mod = jax.nn.silu(c) @ w_ada[l] + b_ada[l]
        sh1, sc1, g1, sh2, sc2, g2 = jnp.split(mod, 6, axis=-1)
        h = rmsnorm(x, pre_mix_gain[l]) * (1.0 + sc1[:, None]) + sh1[:, None]
        y = token_mixer(h, w_in[l], lambda_q1[l], lambda_k1[l], lambda_q2[l], lambda_k2[l],
                        diff_head_gain[l], w_out[l], rel_bias, lambda_init)
        x = x + g1[:, None] * rmsnorm(y, post_mix_gain[l])
        h = rmsnorm(x, pre_ffn_gain[l]) * (1.0 + sc2[:, None]) + sh2[:, None]
        y = hier_moe(h.reshape(b * s, d), w_group[l], b_group[l], w_expert[l], b_expert[l],
                     w_gate[l], w_up[l], w_down[l]).reshape(b, s, d)
        x = x + g2[:, None] * rmsnorm(y, post_ffn_gain[l])
    return x


_drawn_inputs = setup_inputs


def setup_inputs(seed=0):
    import zlib

    import numpy as np

    out = dict(_drawn_inputs(seed))
    spreads = {}
    factors = {'post_ffn_gain': 4.15,
     'lambda_q1': 8.0,
     'lambda_k1': 2.767,
     'b_group': 3.262,
     'b_expert': 2.959}
    for name, (base, spread) in spreads.items():
        noise = np.random.default_rng([zlib.crc32(name.encode()), seed]).standard_normal(out[name].shape)
        drawn = base * np.exp(spread * noise) if base else spread * noise
        out[name] = jnp.asarray(drawn.astype(out[name].dtype))
    for name, factor in factors.items():
        out[name] = (out[name] * factor).astype(out[name].dtype)
    return out
```

```python
import math
from contextlib import ExitStack

import concourse.bass as bass
from concourse import mybir

P = 128
SEQ, D = 256, 1024
TT = SEQ // P
DC = D // P
HEAD = 64
N_DIFF, N_MOBA = 4, 8
N_BIAS = N_DIFF + N_MOBA
PAIRS = N_DIFF + N_MOBA // 2
N_BUCKETS, MAX_DISTANCE = 32, 128
N_GROUPS, PER_GROUP = 4, 8
N_EXPERTS = N_GROUPS * PER_GROUP
FF = D // 2
FC = FF // P
EPS, NEG = 1e-6, -1e30
LAMBDA_INIT = 0.8 - 0.6 * math.exp(-0.3 * 0)

UW = 2048
RING = 12
UPE = 6
SPLITS = 3
SLOTS = 64
PASSES = SEQ // SLOTS


def prologue_units():
    units = [("ada", 0, k) for k in range(DC)]
    ada2 = [("ada", a, k) for a in (1, 2) for k in range(DC)]
    for b in range(6):
        units += [("win", b, 0), ("win", b, 1)]
        n = 3 if b < 4 else 2
        units += ada2[:n]
        ada2 = ada2[n:]
    return units + [("wout", u, 0) for u in range(4)]


UNITS = prologue_units()
BASE = len(UNITS)
UNIT_AT = {u: n for n, u in enumerate(UNITS)}
ADA_ORDER = [u for u in UNITS if u[0] == "ada"]


def slot_of(n):
    return n % RING


def uses_of(n):
    return n // RING + 1


def buckets():
    exact = N_BUCKETS // 2

    def bucket(d):
        if d < exact:
            return d
        return min(exact + int(math.log(d / exact) / math.log(MAX_DISTANCE / exact) * (N_BUCKETS - exact)),
                   N_BUCKETS - 1)

    out = []
    for d in range(SEQ):
        if out and out[-1][2] == bucket(d):
            out[-1][1] = d
        else:
            out.append([d, d, bucket(d)])
    return out


def build(nc, x, c, w_ada, b_ada, pre_mix_gain, post_mix_gain, pre_ffn_gain, post_ffn_gain, w_in,
          lambda_q1, lambda_k1, lambda_q2, lambda_k2, diff_head_gain, w_out, rel_bias,
          w_group, b_group, w_expert, b_expert, w_gate, w_up, w_down, out):
    f32, f32r, i32 = mybir.dt.float32, mybir.dt.float32r, mybir.dt.int32
    ALU, ACT, AX = mybir.AluOpType, mybir.ActivationFunctionType, mybir.AxisListType

    ctx = ExitStack()
    with ctx:
        def sb(name, shape, dt=f32, at=ctx):
            return at.enter_context(nc.sbuf_tensor(name, shape, dt))

        def sem(name):
            return ctx.enter_context(nc.semaphore(name))

        W = sb("W", [P, RING, UW])
        X = sb("X", [P, TT, D])
        Hn = sb("Hn", [P, TT, D])
        G2 = sb("G2", [P, D])
        ident = sb("ident", [P, P])
        ones = sb("ones", [P, P])
        stack2 = sb("stack2", [P, SLOTS])
        before = sb("before", [P, P])
        slot_no = sb("slot_no", [P, 2 * SLOTS])
        num32 = sb("num32", [P, TT, N_EXPERTS])
        cT = sb("cT", [P, DC])
        cS = sb("cS", [P, DC])
        st = sb("st", [P, 64])
        epsb = sb("epsb", [P, 1])
        hgain = sb("hgain", [P, 1])
        wr = sb("wr", [P, DC, N_GROUPS + N_EXPERTS])
        brow = sb("brow", [1, N_GROUPS + N_EXPERTS])
        LE = N_EXPERTS + 2
        PG = sb("PG", [P, LE, 2, TT])
        posm = PG[:, :, 0, :].rearrange("p e t -> p t e")
        gates = PG[:, :, 1, :].rearrange("p e t -> p t e")
        cur = sb("cur", [P, 2, 2, TT])
        maxcnt = sb("maxcnt", [1, 1], i32)
        rt = sb("rt", [P, 10, TT, N_EXPERTS])
        logits = sb("logits", [P, TT, N_GROUPS + N_EXPERTS])

        early = ExitStack()
        MOD = sb("MOD", [P, 5 * D], at=early)
        MODG = sb("MODG", [P, D], at=early)
        gain = sb("gain", [P, 3, D], at=early)
        hT = sb("hT", [P, DC, SEQ], at=early)
        qkT = sb("qkT", [P, 16, SEQ], at=early)
        toe = sb("toe", [P, N_BIAS, SEQ], at=early)
        S = sb("S", [P, 2, 2, 3 * P], at=early)
        PT = sb("PT", [P, 2, 3 * P], at=early)
        tabT = sb("tabT", [N_BIAS, N_BUCKETS], at=early)
        line = sb("line", [N_BIAS, 3 * P], at=early)
        flip = sb("flip", [P, P], at=early)
        lams = sb("lams", [P, 4, HEAD], at=early)
        early.close()
        sq = MOD[:, 0:D]
        rs = MOD[:, D:2 * D]

        WH = sb("WH", [P, SPLITS, UW], f32r)
        WL = sb("WL", [P, SPLITS, UW], f32r)
        XT = sb("XT", [P, 2, DC, 2, SLOTS], f32r)
        GU = sb("GU", [P, 2 * FF])
        SG = sb("SG", [P, FC * SLOTS])
        HID = sb("HID", [P, FC, SLOTS])
        HT = sb("HT", [P, FC, 2, SLOTS], f32r)
        YH = sb("YH", [P, D], f32r)
        YL = sb("YL", [P, D], f32r)
        OH = sb("OH", [P, 2, TT, 2 * SLOTS])
        OG = sb("OG", [P, 2, TT, 2 * SLOTS])
        ST = sb("ST", [P, 2, SEQ], f32r)
        gcol = sb("gcol", [P, 2])
        junk = W[:, 0, 0:D]

        PS = ctx.enter_context(nc.psum_tensor("PS", [P, 8, 512], f32))
        ACC = PS[:, 4:8, :].rearrange("p (t n) f -> p t (n f)", t=TT)

        line_dram = nc.dram_tensor("line_dram", [N_BIAS, 3 * P], f32).ap()

        unit_in = [sem(f"unit_in{s}") for s in range(RING)]
        ada_used, win_used = sem("ada_used"), sem("win_used")
        c_in, x_in, ada_b_in, gain_in, tab_in, lam_in = (sem(n) for n in ("c_in", "x_in", "ada_b_in", "gain_in", "tab_in", "lam_in"))
        router_in, hgain_in, line_out, toe_in = (sem(n) for n in ("router_in", "hgain_in", "line_out", "toe_in"))
        mod_zero, consts, table_set, pool_step = (sem(n) for n in ("mod_zero", "consts", "table_set", "pool_step"))
        c_silu, toe_mm, toe_ready, mod_mm, mod_row = (sem(n) for n in ("c_silu", "toe_mm", "toe_ready", "mod_mm", "mod_row"))
        stat_sq, stat_std, stat_inv = sem("stat_sq"), sem("stat_std"), sem("stat_inv")
        h_ready, hT_mm, hT_ready = sem("h_ready"), sem("hT_mm"), sem("hT_ready")
        proj_ready, lam_sum, lam_exp, lam_ready = (sem(n) for n in ("proj_ready", "lam_sum", "lam_exp", "lam_ready"))
        score_mm, score_read, negmax, exp_ready, prob_ready = (sem(n) for n in ("score_mm", "score_read", "negmax", "exp_ready", "prob_ready"))
        pt_mm, pt_ready, pv_mm, y_ready = (sem(n) for n in ("pt_mm", "pt_ready", "pv_mm", "y_ready"))
        sq_mm, rms_ready, ydiff_ready = sem("sq_mm"), sem("rms_ready"), sem("ydiff_ready")
        out_mm, x2_ready, logit_mm, dve_step = (sem(n) for n in ("out_mm", "x2_ready", "logit_mm", "dve_step"))
        group_sub, group_exp, pair_sub, pair_exp = (sem(n) for n in ("group_sub", "group_exp", "pair_sub", "pair_exp"))
        routed, pos_mm, placed, acc_zeroed = (sem(n) for n in ("routed", "pos_mm", "placed", "acc_zeroed"))
        hi_ready, lo_ready, split_used = sem("hi_ready"), sem("lo_ready"), sem("split_used")
        onehot_ready, prep_mm, gather_mm, scatT_ready, xh_ready, xl_ready = (
            sem(n) for n in ("onehot_ready", "prep_mm", "gather_mm", "scatT_ready", "xh_ready", "xl_ready"))
        gu_read, gt_mm, silu_ready, hid_ready, hh_ready, hl_ready = (
            sem(n) for n in ("gu_read", "gt_mm", "silu_ready", "hid_ready", "hh_ready", "hl_ready"))
        yh_ready, yl_ready, scat_mm = sem("yh_ready"), sem("yl_ready"), sem("scat_mm")
        cur_ready, pass_shift, final_row, stored = sem("cur_ready"), sem("pass_shift"), sem("final_row"), sem("stored")

        block = ctx.enter_context(nc.Block())

        def by_pairs(eng, pair):
            pair(0)
            with eng.Fori(1, N_EXPERTS // 2) as i:
                pair(i)

        def all_passes(eng, one_pass):
            one_pass(0)
            most = eng.value_load(maxcnt[0:1, 0:1], min_val=0, max_val=SEQ)
            for p in range(1, PASSES):
                with eng.If(most > SLOTS * p):
                    one_pass(p)

        def experts_before(i, odd, p):
            return i * 2 + (odd + N_EXPERTS * p)

        def preparations_before(i, odd, p):
            return i * 2 + (odd + (N_EXPERTS + 1) * p)

        def units_before(i, odd, p, u):
            return i * (2 * UPE) + (UPE * odd + u + N_EXPERTS * UPE * p)

        def is_first(i, odd):
            return isinstance(i, int) and i == 0 and odd == 0

        def ring_slot(odd, u):
            return slot_of(BASE + UPE * odd + u)

        def unit_source(e, u):
            if u < 4:
                w = (w_gate, w_up)[u // 2]
                v = w.rearrange("l e (h k p) f -> h (l e) p k f", p=P, h=2)[u % 2]
            else:
                v = w_down.rearrange("l e (h k p) f -> h (l e) p k f", p=P, h=2)[u - 4]
            return v[bass.ds(e, 1)].rearrange("a p k f -> p (a k) f")

        @block.sync
        def _(sp):
            def load(n, source):
                k = source.shape[1]
                sp.dma_start(W[:, slot_of(n), :].rearrange("p (k f) -> p k f", k=k), source).then_inc(unit_in[slot_of(n)], 16)

            def wait_reader(n):
                kind, a, b = UNITS[n]
                if kind == "ada":
                    sp.wait_ge(ada_used, ADA_ORDER.index(UNITS[n]) + 1)
                elif kind == "win":
                    sp.wait_ge(win_used, a + 1)
                else:
                    sp.wait_ge(out_mm, TT)

            for n, (kind, a, b) in enumerate(UNITS):
                if n >= RING:
                    wait_reader(n - RING)
                if kind == "ada":
                    load(n, w_ada[0, b * P:(b + 1) * P, a * UW:(a + 1) * UW].rearrange("p (k f) -> p k f", k=1))
                elif kind == "win":
                    load(n, w_in[0].rearrange("(h k p) n -> h p k n", h=2, p=P)[b][:, :, a * 512:(a + 1) * 512])
                else:
                    load(n, w_out[0].rearrange("(h k p) n -> h p k n", h=4, p=P)[a])

            def stream(p):
                first = 32 * p * UPE
                for u in range(2 * UPE):
                    if p == 0:
                        wait_reader(BASE + u - RING)
                    else:
                        sp.wait_ge(lo_ready, first + u + 1 - RING)
                    load(BASE + first + u, unit_source(u // UPE, u % UPE))
                with sp.Fori(1, N_EXPERTS // 2) as i:
                    for u in range(2 * UPE):
                        sp.wait_ge(lo_ready, i * (2 * UPE) + (first + u + 1 - RING))
                        load(BASE + u, unit_source(i * 2 + u // UPE, u % UPE))

            stream(0)
            sp.wait_ge(placed, 1)
            most = sp.value_load(maxcnt[0:1, 0:1], min_val=0, max_val=SEQ)
            for p in range(1, PASSES):
                with sp.If(most > SLOTS * p):
                    stream(p)
            out_v = out[0].rearrange("(t p) d -> p t d", p=P)
            for t in range(TT):
                sp.wait_ge(final_row, t + 1)
                sp.dma_start(out_v[:, t, :], Hn[:, t, :]).then_inc(stored, 16)
            sp.wait_ge(stored, 16 * TT)

        @block.gpsimd
        def _(pool):
            nc.gpsimd.memset(MOD[:], 0.0).then_inc(mod_zero, 1)
            nc.gpsimd.memset(MODG[:], 0.0).then_inc(mod_zero, 1)
            nc.gpsimd.memset(ones[:], 1.0).then_inc(pool_step, 1)
            nc.gpsimd.memset(epsb[:], EPS).then_inc(consts, 1)
            pool.wait_ge(pool_step, 1)
            nc.gpsimd.affine_select(out=ident[:], in_=ones[:], compare_op=ALU.is_equal, fill=0.0, base=0,
                                    pattern=[[-1, P]], channel_multiplier=1).then_inc(consts, 1)
            nc.gpsimd.affine_select(out=flip[:], in_=ones[:], compare_op=ALU.is_equal, fill=0.0, base=1 - P,
                                    pattern=[[1, P]], channel_multiplier=1).then_inc(consts, 1)
            nc.gpsimd.affine_select(out=before[:], in_=ones[:], compare_op=ALU.is_gt, fill=0.0, base=0,
                                    pattern=[[1, P]], channel_multiplier=-1).then_inc(consts, 1)
            nc.gpsimd.iota(slot_no[:], pattern=[[0, 2], [1, SLOTS]], base=0, channel_multiplier=0,
                           allow_small_or_imprecise_dtypes=True).then_inc(consts, 1)
            nc.gpsimd.iota(num32[:], pattern=[[0, TT], [1, N_EXPERTS]], base=-64, channel_multiplier=0,
                           allow_small_or_imprecise_dtypes=True).then_inc(consts, 1)
            pool.wait_ge(consts, 2)
            nc.gpsimd.tensor_tensor(stack2[:], ident[:, 0:SLOTS], ident[:, SLOTS:P], ALU.add).then_inc(consts, 1)
            nc.gpsimd.memset(line[:], NEG).then_inc(pool_step, 1)
            pool.wait_ge(pool_step, 2)
            pool.wait_ge(tab_in, 16)
            spread = buckets()
            for lo, hi, b in spread:
                nc.gpsimd.tensor_scalar(line[:, 255 - hi:256 - lo], ones[0:N_BIAS, 0:1].to_broadcast([N_BIAS, hi - lo + 1]),
                                        tabT[:, b:b + 1], None, ALU.mult).then_inc(table_set, 1)
            pool.wait_ge(table_set, len(spread))
            pool.dma_start(line_dram, line[:]).then_inc(line_out, 16)
            pool.wait_ge(line_out, 16)
            pool.dma_start(toe[:], bass.AP(line_dram.tensor, 0, [[1, P], [3 * P, N_BIAS], [1, SEQ]])).then_inc(toe_in, 16)

            def column(e, buf):
                nc.gpsimd.tensor_copy(cur[:, buf, :, :], PG[:, bass.ds(e, 1), :, :].rearrange("p e a t -> p (e a) t")).then_inc(cur_ready, 1)

            def prepare(e, buf, m, done):
                pool.wait_ge(cur_ready, m)
                if not isinstance(done, int) or done:
                    pool.wait_ge(onehot_ready, done * 4)
                column(e + 1, 1 - buf)
                for t in range(TT):
                    nc.gpsimd.tensor_scalar(OH[:, buf, t, :], slot_no[:], cur[:, buf, 0, t:t + 1], None,
                                            ALU.is_equal).then_inc(onehot_ready, 1)
                    nc.gpsimd.tensor_scalar(OG[:, buf, t, :], slot_no[:], cur[:, buf, 0, t:t + 1],
                                            cur[:, buf, 1, t:t + 1], ALU.is_equal, ALU.mult).then_inc(onehot_ready, 1)

            def one_pass(p):
                at = (N_EXPERTS + 2) * p
                if p == 0:
                    pool.wait_ge(placed, 1)
                else:
                    pool.wait_ge(pass_shift, p)
                    pool.wait_ge(gather_mm, (N_EXPERTS + 1) * p)
                    pool.wait_ge(cur_ready, at)
                column(0, 0)
                prepare(0, 0, at + 1, (N_EXPERTS + 1) * p)
                prepare(1, 1, at + 2, (N_EXPERTS + 1) * p + 1)
                with pool.Fori(1, N_EXPERTS // 2) as i:
                    for odd in (0, 1):
                        pool.wait_ge(gather_mm, i * 2 + (odd - 1 + (N_EXPERTS + 1) * p))
                        prepare(i * 2 + odd, odd, i * 2 + (odd + 1 + at), i * 2 + (odd + (N_EXPERTS + 1) * p))
                pool.wait_ge(gather_mm, N_EXPERTS - 1 + (N_EXPERTS + 1) * p)
                prepare(N_EXPERTS, 0, at + N_EXPERTS + 1, N_EXPERTS + (N_EXPERTS + 1) * p)

            all_passes(pool, one_pass)

        @block.scalar
        def _(act):
            def broadcast(row, n):
                return bass.AP(row.tensor, row.offset, [[0, P], [1, n]])

            with nc.allow_non_contiguous_dma(reason="small columns"):
                act.dma_start(cT[:], c.rearrange("b (k p) -> p (b k)", p=P)).then_inc(c_in, 16)
                act.dma_start(X[:], x[0].rearrange("(t p) d -> p t d", p=P)).then_inc(x_in, 16)
                act.dma_start(tabT[:], rel_bias.rearrange("b h -> h b")).then_inc(tab_in, 16)
                act.wait_ge(mod_zero, 2)
                act.dma_start(MOD[0:1, :], b_ada[:, 0:5 * D]).then_inc(ada_b_in, 16)
                act.dma_start(MODG[0:1, :], b_ada[:, 5 * D:6 * D]).then_inc(ada_b_in, 16)
                for n, row in enumerate((pre_mix_gain, post_mix_gain, pre_ffn_gain)):
                    act.dma_start(gain[:, n, :], broadcast(row, D)).then_inc(gain_in, 16)
                act.dma_start(G2[:], broadcast(post_ffn_gain, D)).then_inc(gain_in, 16)
                for n, row in enumerate((lambda_q1, lambda_q2, lambda_k1, lambda_k2)):
                    act.dma_start(lams[:, n, :], broadcast(row, HEAD)).then_inc(lam_in, 16)
                act.dma_start(hgain[:], diff_head_gain.rearrange("l d -> d l")).then_inc(hgain_in, 16)
                act.dma_start(wr[:, :, 0:N_GROUPS], w_group[0].rearrange("(k p) n -> p k n", p=P)).then_inc(router_in, 16)
                act.dma_start(wr[:, :, N_GROUPS:], w_expert[0].rearrange("(k p) n -> p k n", p=P)).then_inc(router_in, 16)
                act.dma_start(brow[:, 0:N_GROUPS], b_group).then_inc(router_in, 16)
                act.dma_start(brow[:, N_GROUPS:], b_expert).then_inc(router_in, 16)

            act.wait_ge(c_in, 16)
            nc.scalar.activation(cS[:], cT[:], ACT.Silu).then_inc(c_silu, 1)

            def root_mean(n, source, squares):
                nc.scalar.activation(squares, source, ACT.Square, accum_out=st[:, n:n + 1]).then_inc(stat_sq, 1)
                act.wait_ge(stat_sq, n + 1)
                nc.scalar.activation(st[:, n:n + 1], st[:, n:n + 1], ACT.Sqrt, bias=epsb[:], scale=1.0 / D).then_inc(stat_std, 1)

            act.wait_ge(x_in, 16)
            act.wait_ge(consts, 1)
            for t in range(TT):
                root_mean(t, X[:, t, :], Hn[:, t, :])
            for b in range(6):
                act.wait_ge(toe_mm, b + 1)
                nc.scalar.copy(toe[:, 2 * b:2 * b + 2, :], PS[:, b, :].rearrange("p (h j) -> p h j", h=2)).then_inc(toe_ready, 1)
            act.wait_ge(mod_mm, 1)
            nc.scalar.copy(MOD[:, 0:D], PS[:, 0:2, :].rearrange("p b f -> p (b f)")).then_inc(mod_row, 1)
            for g in range(4):
                act.wait_ge(hT_mm, g + 1)
                nc.scalar.copy(hT[:, 4 * (g % 2):4 * (g % 2) + 4, (g // 2) * P:(g // 2 + 1) * P],
                               PS[:, 4 + g, :].rearrange("p (k t) -> p k t", k=4)).then_inc(hT_ready, 1)
            for b in range(6):
                act.wait_ge(win_used, b + 1)
                two = PS[:, 2 * (b % 2):2 * (b % 2) + 2, :]
                if b in (2, 5):
                    nc.scalar.copy(Hn[:, :, (b // 3) * 512:(b // 3) * 512 + 512], two).then_inc(proj_ready, 1)
                else:
                    chunk = {0: 0, 1: 4, 3: 8, 4: 12}[b]
                    nc.scalar.mul(qkT[:, chunk:chunk + 4, :], two.rearrange("p b (s t) -> p (b s) t", t=SEQ),
                                  HEAD ** -0.5 if b in (0, 3) else 1.0).then_inc(proj_ready, 1)
            act.wait_ge(mod_mm, 2)
            nc.scalar.copy(MOD[:, 3 * D:4 * D], PS[:, 6:8, :].rearrange("p b f -> p (b f)")).then_inc(mod_row, 1)
            act.wait_ge(lam_sum, 1)
            nc.scalar.activation(st[:, 10:12], st[:, 8:10], ACT.Exp).then_inc(lam_exp, 1)

            def exps(g):
                act.wait_ge(negmax, 2 * (g + 1))
                for m in range(2):
                    for t, cols in ((0, slice(0, P)), (1, slice(P, 3 * P))):
                        col = 16 + 8 * (g % 2) + 2 * t + m
                        nc.scalar.activation(S[:, g % 2, m, cols], S[:, g % 2, m, cols], ACT.Exp,
                                             bias=st[:, col:col + 1],
                                             accum_out=st[:, col + 4:col + 5]).then_inc(exp_ready, 1)

            exps(0)
            for g in range(PAIRS):
                if g + 1 < PAIRS:
                    exps(g + 1)
                act.wait_ge(pt_mm, g + 1)
                if g:
                    act.wait_ge(pv_mm, g)
                maps = 1 if g < N_DIFF else 2
                nc.scalar.copy(PT[:, 0:maps, :], PS[:, 4:4 + maps, 0:3 * P]).then_inc(pt_ready, 1)
                act.wait_ge(pv_mm, g + 1)
                nc.scalar.copy(hT[:, g, :], PS[:, 6 + g % 2, 0:SEQ]).then_inc(y_ready, 1)
                if g < N_DIFF:
                    nc.scalar.activation(sq[:, g * SEQ:(g + 1) * SEQ], PS[:, 6 + g % 2, 0:SEQ], ACT.Square).then_inc(y_ready, 1)
            act.wait_ge(sq_mm, 1)
            nc.scalar.activation(rs, PS[:, 0:2, :].rearrange("p b f -> p (b f)"), ACT.Sqrt, bias=epsb[:],
                                 scale=1.0 / (2 * HEAD)).then_inc(rms_ready, 1)
            act.wait_ge(out_mm, TT)
            for t in range(TT):
                root_mean(2 + t, ACC[:, t, :], Hn[:, t, :])
            for t in range(TT):
                act.wait_ge(x2_ready, t + 1)
                root_mean(4 + t, X[:, t, :], Hn[:, t, :])
            for g in range(4):
                act.wait_ge(hT_mm, 4 + g + 1)
                nc.scalar.copy(hT[:, 4 * (g % 2):4 * (g % 2) + 4, (g // 2) * P:(g // 2 + 1) * P],
                               PS[:, g, :].rearrange("p (k t) -> p k t", k=4)).then_inc(hT_ready, 1)
            act.wait_ge(group_sub, 1)
            nc.scalar.activation(rt[:, 0, :, 0:N_GROUPS], rt[:, 0, :, 0:N_GROUPS], ACT.Exp).then_inc(group_exp, 1)
            act.wait_ge(pair_sub, 1)
            nc.scalar.activation(st[:, 44:46], st[:, 44:46], ACT.Exp).then_inc(pair_exp, 1)
            act.wait_ge(pos_mm, 1)

            def one_pass(p):
                def split_high(i, odd, u):
                    n = units_before(i, odd, p, u)
                    ready = 16 * uses_of(BASE + UPE * odd + u) + 16 * (N_EXPERTS // 2) * p
                    act.wait_ge(unit_in[ring_slot(odd, u)], i * 16 + ready)
                    if not is_first(i, odd) or u >= SPLITS or p:
                        act.wait_ge(split_used, n + (1 - SPLITS))
                    nc.scalar.copy(WH[:, u % SPLITS, :], W[:, ring_slot(odd, u), :]).then_inc(hi_ready, 1)

                def output_high(buf, units):
                    act.wait_ge(split_used, units)
                    nc.scalar.mul(YH[:], PS[:, 2:4, :].rearrange("p b f -> p (b f)"),
                                  gcol[:, buf:buf + 1]).then_inc(yh_ready, 1)

                def prepare(buf, m):
                    act.wait_ge(prep_mm, m)
                    nc.scalar.copy(ST[:, buf, :], PS[:, 2, 0:SEQ]).then_inc(scatT_ready, 1)
                    nc.scalar.copy(gcol[:, buf:buf + 1], PS[:, 2, SEQ:SEQ + 1]).then_inc(scatT_ready, 1)
                    act.wait_ge(gather_mm, m)
                    nc.scalar.copy(XT[:, buf, :, 0, :], PS[:, 3, :].rearrange("p (k s) -> p k s", k=DC)).then_inc(xh_ready, 1)

                prepare(0, (N_EXPERTS + 1) * p + 1)

                def pair(i):
                    for odd in (0, 1):
                        n = experts_before(i, odd, p)
                        split_high(i, odd, 0)
                        split_high(i, odd, 1)
                        if not is_first(i, odd):
                            output_high(1 - odd, units_before(i, odd, p, 0))
                        split_high(i, odd, 2)
                        split_high(i, odd, 3)
                        split_high(i, odd, 4)
                        act.wait_ge(split_used, units_before(i, odd, p, 4))
                        nc.scalar.copy(GU[:], PS[:, 0:2, :].rearrange("p b f -> p (b f)")).then_inc(gu_read, 1)
                        split_high(i, odd, 5)
                        act.wait_ge(gt_mm, n + 1)
                        nc.scalar.activation(SG[:], PS[:, 0, 0:FC * SLOTS], ACT.Silu).then_inc(silu_ready, 1)
                        act.wait_ge(hid_ready, n + 1)
                        nc.scalar.copy(HT[:, :, 0, :], HID[:]).then_inc(hh_ready, 1)
                        prepare(1 - odd, preparations_before(i, odd, p) + 2)

                by_pairs(act, pair)
                output_high(1, UPE * N_EXPERTS * (p + 1))

            act.wait_ge(placed, 1)
            all_passes(act, one_pass)
            act.wait_ge(scat_mm, N_EXPERTS)
            for t in range(TT):
                root_mean(6 + t, ACC[:, t, :], junk)

        @block.vector
        def _(dve):
            steps = [0]

            def link(ins):
                steps[0] += 1
                ins.then_inc(dve_step, 1)
                dve.wait_ge(dve_step, steps[0])

            def ada(n):
                _, a, k = ADA_ORDER[n]
                at = UNIT_AT[ADA_ORDER[n]]
                dve.wait_ge(unit_in[slot_of(at)], 16 * uses_of(at))
                if n:
                    dve.wait_ge(ada_used, n)
                if a < 2:
                    m = MOD[:, a * UW:(a + 1) * UW]
                    nc.vector.scalar_tensor_tensor(m, W[:, slot_of(at), :], cS[:, k:k + 1], m,
                                                   ALU.mult, ALU.add).then_inc(ada_used, 1)
                else:
                    link(nc.vector.scalar_tensor_tensor(MOD[:, 4 * D:5 * D], W[:, slot_of(at), 0:D], cS[:, k:k + 1],
                                                        MOD[:, 4 * D:5 * D], ALU.mult, ALU.add))
                    nc.vector.scalar_tensor_tensor(MODG[:], W[:, slot_of(at), D:2 * D], cS[:, k:k + 1],
                                                   MODG[:], ALU.mult, ALU.add).then_inc(ada_used, 1)

            dve.wait_ge(c_silu, 1)
            dve.wait_ge(ada_b_in, 32)
            dve.wait_ge(mod_zero, 2)
            for n in range(DC):
                ada(n)

            def inverse(n):
                dve.wait_ge(stat_std, n + 1)
                nc.vector.reciprocal(st[:, 48 + n:49 + n], st[:, n:n + 1]).then_inc(stat_inv, 1)

            def modulate(t, scale, shift, n):
                dve.wait_ge(stat_inv, n + 1)
                link(nc.vector.scalar_tensor_tensor(Hn[:, t, :], X[:, t, :], st[:, 48 + n:49 + n], scale, ALU.mult, ALU.mult))
                nc.vector.tensor_tensor(Hn[:, t, :], Hn[:, t, :], shift, ALU.add).then_inc(h_ready, 1)

            inverse(0)
            inverse(1)
            dve.wait_ge(gain_in, 64)
            dve.wait_ge(mod_mm, 1)
            link(nc.vector.scalar_tensor_tensor(MOD[:, D:2 * D], PS[:, 2:4, :].rearrange("p b f -> p (b f)"), 1.0, gain[:, 0, :],
                                                ALU.add, ALU.mult))
            dve.wait_ge(mod_row, 1)
            for t in range(TT):
                modulate(t, MOD[:, D:2 * D], MOD[:, 0:D], t)

            for n in range(DC, 3 * DC):
                ada(n)

            dve.wait_ge(lam_in, 64)
            link(nc.vector.tensor_tensor(lams[:, 0:2, :], lams[:, 0:2, :], lams[:, 2:4, :], ALU.mult))
            nc.vector.tensor_reduce(st[:, 8:10], lams[:, 0:2, :], AX.X, ALU.add).then_inc(lam_sum, 1)
            dve.wait_ge(lam_exp, 1)
            link(nc.vector.tensor_tensor(st[:, 12:13], st[:, 11:12], st[:, 10:11], ALU.subtract))
            link(nc.vector.tensor_scalar(st[:, 13:14], st[:, 12:13], -LAMBDA_INIT, None, ALU.add))
            dve.wait_ge(hgain_in, 16)
            link(nc.vector.tensor_scalar(hgain[:], hgain[:], 1.0 - LAMBDA_INIT, None, ALU.mult))
            dve.wait_ge(mod_mm, 2)
            nc.vector.tensor_tensor(MOD[:, 2 * D:3 * D], PS[:, 4:6, :].rearrange("p b f -> p (b f)"), gain[:, 1, :],
                                    ALU.mult).then_inc(mod_row, 1)
            dve.wait_ge(mod_mm, 3)
            nc.vector.scalar_tensor_tensor(MOD[:, 4 * D:5 * D], PS[:, 0:2, :].rearrange("p b f -> p (b f)"), 1.0, gain[:, 2, :],
                                           ALU.add, ALU.mult).then_inc(mod_row, 1)
            nc.vector.tensor_tensor(G2[:], PS[:, 2:4, :].rearrange("p b f -> p (b f)"), G2[:], ALU.mult).then_inc(mod_row, 1)

            dve.wait_ge(toe_ready, 6)

            def scores(g):
                if g >= 2:
                    dve.wait_ge(pt_mm, g - 1)
                dve.wait_ge(score_mm, g + 1)
                b = 2 * (g % 2)
                s0 = 16 + 8 * (g % 2)
                for t, cols, j in ((0, slice(0, P), slice(P, 2 * P)), (1, slice(P, 3 * P), slice(0, 2 * P))):
                    if g < N_DIFF:
                        bias = toe[:, g:g + 1, j].to_broadcast([P, 2, j.stop - j.start])
                    else:
                        h = N_DIFF + 2 * (g - N_DIFF)
                        bias = toe[:, h:h + 2, j]
                    nc.vector.tensor_tensor(S[:, g % 2, :, cols], PS[:, b:b + 2, cols], bias, ALU.add).then_inc(score_read, 1)
                for t, cols in ((0, slice(0, P)), (1, slice(P, 3 * P))):
                    dve.wait_ge(score_read, 2 * g + 1 + t)
                    nc.vector.tensor_reduce(st[:, s0 + 2 * t:s0 + 2 * t + 2], S[:, g % 2, :, cols], AX.X, ALU.max,
                                            negate=True).then_inc(negmax, 1)

            def probabilities(g):
                dve.wait_ge(exp_ready, 4 * (g + 1))
                s0 = 16 + 8 * (g % 2)
                inv = 32 + 4 * (g % 2)
                link(nc.vector.reciprocal(st[:, inv:inv + 4], st[:, s0 + 4:s0 + 8]))
                if g < N_DIFF:
                    for t in range(2):
                        nc.vector.tensor_tensor(st[:, 40 + t:41 + t], st[:, inv + 2 * t + 1:inv + 2 * t + 2], st[:, 13:14], ALU.mult)
                    link(nc.vector.tensor_tensor(st[:, 42:43], st[:, 13:14], st[:, 13:14], ALU.mult))
                for t, cols in ((0, slice(0, P)), (1, slice(P, 3 * P))):
                    for m in range(2):
                        e = S[:, g % 2, m, cols]
                        r = st[:, inv + 2 * t + m:inv + 2 * t + m + 1]
                        if g < N_DIFF and m == 1:
                            r = st[:, 40 + t:41 + t]
                        ins = nc.vector.tensor_scalar(e, e, r, None, ALU.mult)
                        if g >= N_DIFF:
                            ins.then_inc(prob_ready, 1)
                        elif m == 1:
                            link(ins)
                    if g < N_DIFF:
                        nc.vector.tensor_tensor(S[:, g % 2, 0, cols], S[:, g % 2, 0, cols], S[:, g % 2, 1, cols],
                                                ALU.add).then_inc(prob_ready, 2)

            scores(0)
            for g in range(PAIRS):
                if g + 1 < PAIRS:
                    scores(g + 1)
                probabilities(g)
            dve.wait_ge(rms_ready, 1)
            link(nc.vector.reciprocal(rs, rs))
            yd = hT[:, 0:N_DIFF, :].rearrange("p h t -> p (h t)")
            nc.vector.scalar_tensor_tensor(yd, yd, hgain[:], rs, ALU.mult, ALU.mult).then_inc(ydiff_ready, 1)
            for t in range(TT):
                inverse(2 + t)
                dve.wait_ge(stat_inv, 3 + t)
                link(nc.vector.scalar_tensor_tensor(Hn[:, t, :], ACC[:, t, :], st[:, 50 + t:51 + t], MOD[:, 2 * D:3 * D],
                                                    ALU.mult, ALU.mult))
                nc.vector.tensor_tensor(X[:, t, :], X[:, t, :], Hn[:, t, :], ALU.add).then_inc(x2_ready, 1)
            for t in range(TT):
                inverse(4 + t)
                modulate(t, MOD[:, 4 * D:5 * D], MOD[:, 3 * D:4 * D], 4 + t)

            R = [rt[:, k, :, :] for k in range(10)]
            L = logits[:]
            G, E = L[:, :, 0:N_GROUPS], L[:, :, N_GROUPS:]
            g4 = lambda k: rt[:, k, :, 0:N_GROUPS]

            def spread(v, n):
                return v.rearrange("p (t o) -> p t o", o=1).to_broadcast([P, TT, n])

            def first_of(vals, most, k, n):
                a, b = rt[:, k, :, 0:n], rt[:, k + 1, :, 0:n]
                link(nc.vector.tensor_tensor(a, vals, spread(most, n), ALU.is_equal))
                link(nc.vector.tensor_tensor(b, a, num32[:, :, 0:n], ALU.mult))
                link(nc.vector.tensor_reduce(st[:, 46:48], b, AX.X, ALU.min))
                link(nc.vector.tensor_tensor(a, num32[:, :, 0:n], spread(st[:, 46:48], n), ALU.is_equal))
                return a

            dve.wait_ge(logit_mm, 1)
            link(nc.vector.tensor_copy(L, PS[:, 0, 0:TT * 36].rearrange("p (t n) -> p t n", t=TT)))
            gm, gw, m1, m2, d, t1 = (st[:, a:a + 2] for a in (32, 34, 36, 38, 44, 40))
            link(nc.vector.tensor_reduce(gm, G, AX.X, ALU.max))
            nc.vector.tensor_tensor(g4(0), G, spread(gm, N_GROUPS), ALU.subtract).then_inc(group_sub, 1)
            gsel = first_of(G, gm, 1, N_GROUPS)
            link(nc.vector.tensor_scalar(g4(3), gsel, -1.0, -NEG, ALU.add, ALU.mult))
            link(nc.vector.tensor_tensor(R[4].rearrange("p t (g j) -> p t g j", g=N_GROUPS),
                                         E.rearrange("p t (g j) -> p t g j", g=N_GROUPS),
                                         g4(3).rearrange("p t (g o) -> p t g o", o=1).to_broadcast([P, TT, N_GROUPS, PER_GROUP]),
                                         ALU.add))
            link(nc.vector.tensor_reduce(m1, R[4], AX.X, ALU.max))
            o1 = first_of(R[4], m1, 5, N_EXPERTS)
            link(nc.vector.scalar_tensor_tensor(R[7], o1, 3.0 * NEG, R[4], ALU.mult, ALU.add))
            link(nc.vector.tensor_reduce(m2, R[7], AX.X, ALU.max))
            nc.vector.tensor_tensor(d, m2, m1, ALU.subtract).then_inc(pair_sub, 1)
            o2 = first_of(R[7], m2, 8, N_EXPERTS)
            dve.wait_ge(group_exp, 1)
            link(nc.vector.tensor_reduce(gw, g4(0), AX.X, ALU.add))
            link(nc.vector.reciprocal(gw, gw))
            dve.wait_ge(pair_exp, 1)
            link(nc.vector.tensor_scalar(t1, d, 1.0, None, ALU.add))
            link(nc.vector.reciprocal(t1, t1))
            link(nc.vector.tensor_tensor(t1, t1, gw, ALU.mult))
            link(nc.vector.tensor_tensor(d, d, t1, ALU.mult))
            link(nc.vector.tensor_tensor(R[6], o1, spread(t1, N_EXPERTS), ALU.mult))
            link(nc.vector.tensor_tensor(R[9], o2, spread(d, N_EXPERTS), ALU.mult))
            link(nc.vector.memset(PG[:], -1.0))
            link(nc.vector.memset(PG[:, :, 1, :], 0.0))
            link(nc.vector.tensor_tensor(gates[:, :, 0:N_EXPERTS], R[6], R[9], ALU.add))
            nc.vector.tensor_tensor(R[0], o1, o2, ALU.add).then_inc(routed, 1)
            dve.wait_ge(routed, 1)
            dve.wait_ge(pos_mm, 1)
            place = PS[:, 1, 0:TT * N_EXPERTS].rearrange("p (t n) -> p t n", t=TT)
            link(nc.vector.scalar_tensor_tensor(R[1], place, 1.0, R[0], ALU.add, ALU.mult))
            link(nc.vector.tensor_scalar(posm[:, :, 0:N_EXPERTS], R[1], -1.0, None, ALU.add))
            nc.vector.tensor_reduce(maxcnt[:], PS[0:1, 1, 64:64 + N_EXPERTS], AX.X, ALU.max).then_inc(placed, 1)

            def one_pass(p):
                if p:
                    dve.wait_ge(onehot_ready, 4 * (N_EXPERTS + 1) * p)
                    nc.vector.tensor_scalar(PG[:, :, 0, :], PG[:, :, 0, :], -float(SLOTS), None, ALU.add).then_inc(pass_shift, 1)

                def split_low(i, odd, u):
                    n = units_before(i, odd, p, u)
                    dve.wait_ge(hi_ready, n + 1)
                    if not is_first(i, odd) or u >= SPLITS or p:
                        dve.wait_ge(split_used, n + (1 - SPLITS))
                    nc.vector.tensor_tensor(WL[:, u % SPLITS, :], W[:, ring_slot(odd, u), :],
                                            WH[:, u % SPLITS, :].bitcast(f32), ALU.subtract).then_inc(lo_ready, 1)

                def output_low(buf, done):
                    dve.wait_ge(yh_ready, done)
                    nc.vector.scalar_tensor_tensor(YL[:], PS[:, 2:4, :].rearrange("p b f -> p (b f)"), gcol[:, buf:buf + 1],
                                                   YH[:].bitcast(f32), ALU.mult, ALU.subtract).then_inc(yl_ready, 1)

                def tokens_low(buf, m):
                    dve.wait_ge(xh_ready, m)
                    nc.vector.tensor_tensor(XT[:, buf, :, 1, :], PS[:, 3, :].rearrange("p (k s) -> p k s", k=DC),
                                            XT[:, buf, :, 0, :].bitcast(f32), ALU.subtract).then_inc(xl_ready, 1)

                tokens_low(0, (N_EXPERTS + 1) * p + 1)

                def pair(i):
                    for odd in (0, 1):
                        n = experts_before(i, odd, p)
                        split_low(i, odd, 0)
                        split_low(i, odd, 1)
                        if not is_first(i, odd):
                            output_low(1 - odd, n)
                        for u in (2, 3, 4, 5):
                            split_low(i, odd, u)
                        dve.wait_ge(silu_ready, n + 1)
                        nc.vector.tensor_tensor(HID[:].rearrange("p k s -> p (k s)"), SG[:], PS[:, 0, FC * SLOTS:],
                                                ALU.mult).then_inc(hid_ready, 1)
                        dve.wait_ge(hh_ready, n + 1)
                        nc.vector.tensor_tensor(HT[:, :, 1, :], HID[:], HT[:, :, 0, :].bitcast(f32),
                                                ALU.subtract).then_inc(hl_ready, 1)
                        tokens_low(1 - odd, preparations_before(i, odd, p) + 2)

                by_pairs(dve, pair)
                output_low(1, N_EXPERTS * (p + 1))
                dve.wait_ge(scat_mm, N_EXPERTS * (p + 1))

            all_passes(dve, one_pass)
            for t in range(TT):
                inverse(6 + t)
                dve.wait_ge(stat_inv, 7 + t)
                link(nc.vector.scalar_tensor_tensor(Hn[:, t, :], ACC[:, t, :], st[:, 54 + t:55 + t], G2[:], ALU.mult, ALU.mult))
                nc.vector.tensor_tensor(Hn[:, t, :], Hn[:, t, :], X[:, t, :], ALU.add).then_inc(final_row, 1)

        @block.tensor
        def _(pe):
            def arrived(unit):
                at = UNIT_AT[unit]
                pe.wait_ge(unit_in[slot_of(at)], 16 * uses_of(at))

            pe.wait_ge(consts, 7)
            pe.wait_ge(toe_in, 16)
            for b in range(6):
                nc.tensor.matmul(PS[:, b, :], flip[:], toe[:, 2 * b:2 * b + 2, :].rearrange("p h j -> p (h j)"),
                                 start=True, stop=True).then_inc(toe_mm, 1)

            def sum_rows(parts, first_bank):
                for b, part in enumerate(parts):
                    last = nc.tensor.matmul(PS[:, first_bank + b, :], ones[:], part, start=True, stop=True)
                last.then_inc(mod_mm, 1)

            def mod_parts(a):
                return [MOD[:, a * D + 512 * b:a * D + 512 * b + 512] for b in range(2)]

            pe.wait_ge(ada_used, DC)
            pe.wait_ge(toe_ready, 6)
            sum_rows(mod_parts(0) + mod_parts(1), 0)

            def transpose_h(first_h, bank):
                for t in range(TT):
                    pe.wait_ge(h_ready, first_h + t + 1)
                    for half in range(2):
                        for k in range(4):
                            last = nc.tensor.transpose(PS[:, bank + 2 * t + half, k * P:(k + 1) * P],
                                                       Hn[:, t, (4 * half + k) * P:(4 * half + k + 1) * P], ident[:])
                        last.then_inc(hT_mm, 1)

            transpose_h(0, 4)
            pe.wait_ge(hT_ready, 4)
            for b in range(6):
                arrived(("win", b, 0))
                arrived(("win", b, 1))
                if b >= 2:
                    pe.wait_ge(proj_ready, b - 1)
                w = [W[:, slot_of(UNIT_AT["win", b, k // 4]), (k % 4) * 512:(k % 4 + 1) * 512] for k in range(DC)]
                bank = 2 * (b % 2)
                if b in (2, 5):
                    for t in range(TT):
                        for k in range(DC):
                            last = nc.tensor.matmul(PS[:, bank + t, :], hT[:, k, t * P:(t + 1) * P], w[k],
                                                    start=(k == 0), stop=(k == DC - 1))
                else:
                    for s in range(4):
                        for k in range(DC):
                            last = nc.tensor.matmul(PS[:, bank + s // 2, (s % 2) * SEQ:(s % 2 + 1) * SEQ],
                                                    w[k][:, s * P:(s + 1) * P], hT[:, k, :],
                                                    start=(k == 0), stop=(k == DC - 1))
                last.then_inc(win_used, 1)
            pe.wait_ge(ada_used, 3 * DC)
            sum_rows(mod_parts(2) + mod_parts(3), 4)
            pe.wait_ge(proj_ready, 6)
            sum_rows(mod_parts(4) + [MODG[:, 0:512], MODG[:, 512:1024]], 0)

            def score(g):
                if g < N_DIFF:
                    q, k = g, 4 + g
                else:
                    q, k = 8 + g - N_DIFF, 12 + g - N_DIFF
                if g == 0:
                    pe.wait_ge(mod_row, 5)
                if g >= 2:
                    pe.wait_ge(score_read, 2 * (g - 1))
                for t in range(TT):
                    for m in range(2):
                        half = slice(64 * m, 64 * m + 64)
                        last = nc.tensor.matmul(PS[:, 2 * (g % 2) + m, (0 if t == 0 else P):(P if t == 0 else 3 * P)],
                                                qkT[half, q, t * P:(t + 1) * P], qkT[half, k, 0:(t + 1) * P],
                                                start=True, stop=True)
                last.then_inc(score_mm, 1)

            def transpose_probabilities(g):
                pe.wait_ge(prob_ready, 4 * (g + 1))
                if g:
                    pe.wait_ge(pt_ready, g)
                for m in range(1 if g < N_DIFF else 2):
                    for n in range(3):
                        last = nc.tensor.transpose(PS[:, 4 + m, n * P:(n + 1) * P], S[:, g % 2, m, n * P:(n + 1) * P], ident[:])
                last.then_inc(pt_mm, 1)

            def weigh_values(g):
                pe.wait_ge(pt_ready, g + 1)
                if g >= 2:
                    pe.wait_ge(y_ready, 2 * (g - 1) if g - 2 < N_DIFF else 2 * N_DIFF + g - 1 - N_DIFF)
                bank = 6 + g % 2
                if g < N_DIFF:
                    jobs = [(0, slice(0, P), Hn[:, 0, g * P:(g + 1) * P], Hn[:, 1, g * P:(g + 1) * P])]
                else:
                    jobs = []
                    for m in range(2):
                        c0 = 512 + (2 * (g - N_DIFF) + m) * HEAD
                        jobs.append((m, slice(64 * m, 64 * m + 64), Hn[:, 0, c0:c0 + HEAD], Hn[:, 1, c0:c0 + HEAD]))
                for m, rows, v0, v1 in jobs:
                    nc.tensor.matmul(PS[rows, bank, 0:SEQ], v0, PT[:, m, 0:SEQ], start=True, stop=False)
                    last = nc.tensor.matmul(PS[rows, bank, P:SEQ], v1, PT[:, m, SEQ:3 * P], start=False, stop=True)
                last.then_inc(pv_mm, 1)

            score(0)
            score(1)
            for g in range(PAIRS):
                transpose_probabilities(g)
                if g + 2 < PAIRS:
                    score(g + 2)
                weigh_values(g)
            pe.wait_ge(y_ready, 2 * N_DIFF + PAIRS - N_DIFF)
            pe.wait_ge(score_read, 2 * PAIRS)
            for b in range(2):
                last = nc.tensor.matmul(PS[:, b, :], ones[:], sq[:, 512 * b:512 * b + 512], start=True, stop=True)
            last.then_inc(sq_mm, 1)
            order = [4, 5, 6, 7, 0, 1, 2, 3]
            for k in order:
                if k == 4:
                    arrived(("wout", 2, 0))
                if k == 6:
                    arrived(("wout", 3, 0))
                if k == 0:
                    pe.wait_ge(ydiff_ready, 1)
                    arrived(("wout", 0, 0))
                if k == 2:
                    arrived(("wout", 1, 0))
                for t in range(TT):
                    for half in range(2):
                        wo = W[:, slot_of(UNIT_AT["wout", k // 2, 0]), (k % 2) * D + half * 512:(k % 2) * D + half * 512 + 512]
                        last = nc.tensor.matmul(PS[:, 4 + 2 * t + half, :], hT[:, k, t * P:(t + 1) * P], wo,
                                                start=(k == order[0]), stop=(k == order[-1]))
            last.then_inc(out_mm, TT)
            transpose_h(2, 0)
            pe.wait_ge(hT_ready, 8)
            pe.wait_ge(router_in, 64)
            for t in range(TT):
                lg = PS[:, 0, t * 36:(t + 1) * 36]
                for k in range(DC):
                    nc.tensor.matmul(lg, hT[:, k, t * P:(t + 1) * P], wr[:, k, :], start=(k == 0), stop=False)
                last = nc.tensor.matmul(lg, ones[0:1, :], brow[0:1, :], start=False, stop=True)
            last.then_inc(logit_mm, 1)
            pe.wait_ge(routed, 1)
            m0, m1 = rt[:, 0, 0, :], rt[:, 0, 1, :]
            E = N_EXPERTS
            nc.tensor.matmul(PS[:, 1, 0:E], before[:], m0, start=True, stop=True)
            nc.tensor.matmul(PS[:, 1, E:2 * E], ones[:], m0, start=True, stop=False)
            nc.tensor.matmul(PS[:, 1, E:2 * E], before[:], m1, start=False, stop=True)
            nc.tensor.matmul(PS[:, 1, 2 * E:3 * E], ones[:], m0, start=True, stop=False)
            nc.tensor.matmul(PS[:, 1, 2 * E:3 * E], ones[:], m1, start=False, stop=True).then_inc(pos_mm, 1)
            pe.wait_ge(placed, 1)

            def one_pass(p):
                def prepare(buf, m):
                    pe.wait_ge(onehot_ready, m * 4)
                    for t in range(TT):
                        nc.tensor.transpose(PS[:, 2, t * P:(t + 1) * P], OH[:, buf, t, :], ident[:])
                    for t in range(TT):
                        last = nc.tensor.matmul(PS[:, 2, SEQ:SEQ + 1], OG[:, buf, t, :], ones[:, 0:1],
                                                start=(t == 0), stop=(t == TT - 1))
                    last.then_inc(prep_mm, 1)
                    for k in range(DC):
                        for t in range(TT):
                            last = nc.tensor.matmul(PS[:, 3, k * SLOTS:(k + 1) * SLOTS], Hn[:, t, k * P:(k + 1) * P],
                                                    OH[:, buf, t, 0:SLOTS], start=(t == 0), stop=(t == TT - 1))
                    last.then_inc(gather_mm, 1)

                def scatter(buf, done, first):
                    pe.wait_ge(yl_ready, done)
                    for t in range(TT):
                        for half in range(2):
                            for y in (YH, YL):
                                last = nc.tensor.matmul(PS[:, 4 + 2 * t + half, :], ST[:, buf, t * P:(t + 1) * P],
                                                        y[:, half * 512:half * 512 + 512],
                                                        start=first and y is YH, stop=True, skip_group_check=True)
                    last.then_inc(scat_mm, 1)

                def unit(i, odd, u, outs):
                    n = units_before(i, odd, p, u)
                    for part, ready in ((WH, hi_ready), (WL, lo_ready)):
                        pe.wait_ge(ready, n + 1)
                        for q in range(4):
                            bank, lhsT, begin, end = outs(q, part is WH)
                            last = nc.tensor.matmul(PS[:, bank, :], lhsT, part[:, u % SPLITS, q * 512:(q + 1) * 512],
                                                    start=begin, stop=end)
                    last.then_inc(split_used, 1)

                prepare(0, (N_EXPERTS + 1) * p + 1)

                def pair(i):
                    for odd in (0, 1):
                        n = experts_before(i, odd, p)
                        m = preparations_before(i, odd, p)
                        pe.wait_ge(xh_ready, m + 1)
                        pe.wait_ge(xl_ready, m + 1)
                        for u in range(4):
                            def into(q, high):
                                k = 4 * (u % 2) + q
                                return (u // 2, XT[:, odd, k, :, :].rearrange("p a s -> p (a s)"),
                                        k == 0 and high, k == DC - 1 and not high)
                            unit(i, odd, u, into)
                        if not is_first(i, odd):
                            scatter(1 - odd, n, isinstance(i, int) and p == 0 and odd == 1)
                        pe.wait_ge(gu_read, n + 1)
                        for q in range(2 * FC):
                            last = nc.tensor.matmul(PS[:, 0, q * SLOTS:(q + 1) * SLOTS], GU[:, q * P:(q + 1) * P], stack2[:],
                                                    start=True, stop=True)
                        last.then_inc(gt_mm, 1)
                        prepare(1 - odd, m + 2)
                        pe.wait_ge(hl_ready, n + 1)
                        pe.wait_ge(scatT_ready, (m + 2) * 2)
                        pe.wait_ge(xl_ready, m + 2)
                        for u in (4, 5):
                            def down(q, high):
                                k = 2 * (u - 4) + q // 2
                                return (2 + q % 2, HT[:, k, :, :].rearrange("p a s -> p (a s)"),
                                        k == 0 and high, k == FC - 1 and not high)
                            unit(i, odd, u, down)

                by_pairs(pe, pair)
                scatter(1, N_EXPERTS * (p + 1), False)

            all_passes(pe, one_pass)


_INS = ["x", "c", "w_ada", "b_ada", "pre_mix_gain", "post_mix_gain", "pre_ffn_gain", "post_ffn_gain", "w_in",
        "lambda_q1", "lambda_k1", "lambda_q2", "lambda_k2", "diff_head_gain", "w_out", "rel_bias",
        "w_group", "b_group", "w_expert", "b_expert", "w_gate", "w_up", "w_down"]
_OUT = ((1, 256, 1024), "float32")


def kernel(**inputs):
    import numpy as _np
    import concourse.bacc as _bacc
    from concourse import mybir as _mybir
    from concourse.bass_utils import run_bass_kernel_spmd as _run

    nc = _bacc.Bacc("TRN2", target_bir_lowering=False, num_devices=1)
    arrays, args = {}, []
    for name in _INS:
        a = _np.ascontiguousarray(inputs[name])
        arrays[f"in_{name}_dram"] = a
        args.append(nc.dram_tensor(f"in_{name}_dram", a.shape, _mybir.dt.from_np(a.dtype), kind="ExternalInput").ap())
    args.append(nc.dram_tensor("out_0_dram", _OUT[0], _mybir.dt.from_np(_np.dtype(_OUT[1])), kind="ExternalOutput").ap())
    build(nc, *args)
    r = _run(nc, [arrays], core_ids=[0])
    return r.results[0]["out_0_dram"]
```

```python
import math
from contextlib import ExitStack

import concourse.bass as bass
from concourse import mybir

P = 128
SEQ, D = 256, 1024
TT = SEQ // P
DC = D // P
HEAD = 64
N_DIFF, N_MOBA = 4, 8
N_BIAS = N_DIFF + N_MOBA
PAIRS = N_DIFF + N_MOBA // 2
N_BUCKETS, MAX_DISTANCE = 32, 128
N_GROUPS, PER_GROUP = 4, 8
N_EXPERTS = N_GROUPS * PER_GROUP
FF = D // 2
FC = FF // P
EPS, NEG = 1e-6, -1e30
LAMBDA_INIT = 0.8 - 0.6 * math.exp(-0.3 * 0)

UW = 2048
RING = 12
UPE = 6
SPLITS = 4
SLOTS = 64
PASSES = SEQ // SLOTS


def prologue_units():
    units = [("ada", 0, k) for k in range(DC)]
    ada2 = [("ada", a, k) for a in (1, 2) for k in range(DC)]
    for b in range(6):
        units += [("win", b, 0), ("win", b, 1)]
        n = 3 if b < 4 else 2
        units += ada2[:n]
        ada2 = ada2[n:]
    return units + [("wout", u, 0) for u in range(4)]


UNITS = prologue_units()
BASE = len(UNITS)
UNIT_AT = {u: n for n, u in enumerate(UNITS)}
ADA_ORDER = [u for u in UNITS if u[0] == "ada"]


def slot_of(n):
    return n % RING


def uses_of(n):
    return n // RING + 1


def buckets():
    exact = N_BUCKETS // 2

    def bucket(d):
        if d < exact:
            return d
        return min(exact + int(math.log(d / exact) / math.log(MAX_DISTANCE / exact) * (N_BUCKETS - exact)),
                   N_BUCKETS - 1)

    out = []
    for d in range(SEQ):
        if out and out[-1][2] == bucket(d):
            out[-1][1] = d
        else:
            out.append([d, d, bucket(d)])
    return out


def build(nc, x, c, w_ada, b_ada, pre_mix_gain, post_mix_gain, pre_ffn_gain, post_ffn_gain, w_in,
          lambda_q1, lambda_k1, lambda_q2, lambda_k2, diff_head_gain, w_out, rel_bias,
          w_group, b_group, w_expert, b_expert, w_gate, w_up, w_down, out):
    f32, f32r, bf16, i32 = mybir.dt.float32, mybir.dt.float32r, mybir.dt.bfloat16, mybir.dt.int32
    ALU, ACT, AX = mybir.AluOpType, mybir.ActivationFunctionType, mybir.AxisListType

    ctx = ExitStack()
    with ctx:
        def sb(name, shape, dt=f32, at=ctx):
            return at.enter_context(nc.sbuf_tensor(name, shape, dt))

        def sem(name):
            return ctx.enter_context(nc.semaphore(name))

        W, WL = [], []
        for slot in range(RING):
            with nc.sbuf_tensor(f"W{slot}", [P, UW], f32) as w:
                W.append(w)
            WL.append(sb(f"WL{slot}", [P, UW], f32r))
        X = sb("X", [P, TT, D])
        Hn = sb("Hn", [P, TT, D])
        G2 = sb("G2", [P, D])
        ident = sb("ident", [P, P])
        ones = sb("ones", [P, P])
        ident16 = sb("ident16", [P, P], bf16)
        stack2 = sb("stack2", [P, SLOTS])
        before = sb("before", [P, P])
        slot_no = sb("slot_no", [P, 2 * SLOTS])
        num32 = sb("num32", [P, TT, N_EXPERTS])
        cT = sb("cT", [P, DC])
        cS = sb("cS", [P, DC])
        st = sb("st", [P, 64])
        epsb = sb("epsb", [P, 1])
        hgain = sb("hgain", [P, 1])
        wr = sb("wr", [P, DC, N_GROUPS + N_EXPERTS])
        brow = sb("brow", [1, N_GROUPS + N_EXPERTS])
        LE = N_EXPERTS + 1
        PG = sb("PG", [P, LE, 2, TT])
        posm = PG[:, :, 0, :].rearrange("p e t -> p t e")
        gates = PG[:, :, 1, :].rearrange("p e t -> p t e")
        cur = sb("cur", [P, 2, 2, TT])
        maxcnt = sb("maxcnt", [1, 1], i32)
        rt = sb("rt", [P, 10, TT, N_EXPERTS])
        logits = sb("logits", [P, TT, N_GROUPS + N_EXPERTS])

        early = ExitStack()
        hT = sb("hT", [P, DC, SEQ], at=early)
        MOD = sb("MOD", [P, 5 * D], at=early)
        MODG = sb("MODG", [P, D], at=early)
        gain = sb("gain", [P, 3, D], at=early)
        qkT = sb("qkT", [P, 16, SEQ], at=early)
        toe = sb("toe", [P, N_BIAS, SEQ], at=early)
        S = sb("S", [P, 2, 2, 3 * P], at=early)
        PT = sb("PT", [P, 2, 3 * P], at=early)
        tabT = sb("tabT", [N_BIAS, N_BUCKETS], at=early)
        line = sb("line", [N_BIAS, 3 * P], at=early)
        flip = sb("flip", [P, P], at=early)
        lams = PT[:, 0, 0:4 * HEAD].rearrange("p (n d) -> p n d", n=4)
        early.close()
        sq = MOD[:, 0:D]
        rs = MOD[:, D:2 * D]

        WH = sb("WH", [P, SPLITS, UW], f32r)
        H3 = sb("H3", [P, 3, TT, D], bf16)
        XT = sb("XT", [P, DC, 2, SLOTS], f32r)
        GU = sb("GU", [P, 2 * FF])
        SG = sb("SG", [P, FC * SLOTS])
        HID = sb("HID", [P, FC, SLOTS])
        HT = sb("HT", [P, FC, 2, SLOTS], f32r)
        YH = sb("YH", [P, D], f32r)
        YL = sb("YL", [P, D], f32r)
        OH = sb("OH", [P, 2, TT, 2 * SLOTS], bf16)
        OG = sb("OG", [P, 2, TT, 2 * SLOTS])
        ST = sb("ST", [P, 2, SEQ], f32r)
        gcol = sb("gcol", [P, 2])
        junk = W[0][:, 0:D]

        PS = ctx.enter_context(nc.psum_tensor("PS", [P, 8, 512], f32))
        ACC = PS[:, 4:8, :].rearrange("p (t n) f -> p t (n f)", t=TT)

        line_dram = nc.dram_tensor("line_dram", [N_BIAS, 3 * P], f32).ap()

        unit_in = [sem(f"unit_in{s}") for s in range(RING)]
        ada_used, win_used = sem("ada_used"), sem("win_used")
        c_in, x_in, ada_b_in, gain_in, tab_in, lam_in = (sem(n) for n in ("c_in", "x_in", "ada_b_in", "gain_in", "tab_in", "lam_in"))
        router_in, hgain_in, line_out, toe_in = (sem(n) for n in ("router_in", "hgain_in", "line_out", "toe_in"))
        mod_zero, consts, table_set, pool_step = (sem(n) for n in ("mod_zero", "consts", "table_set", "pool_step"))
        c_silu, toe_mm, toe_ready, mod_mm, mod_row = (sem(n) for n in ("c_silu", "toe_mm", "toe_ready", "mod_mm", "mod_row"))
        stat_sq, stat_std, stat_inv = sem("stat_sq"), sem("stat_std"), sem("stat_inv")
        h_ready, hT_mm, hT_ready = sem("h_ready"), sem("hT_mm"), sem("hT_ready")
        proj_ready, lam_sum, lam_exp, lam_ready = (sem(n) for n in ("proj_ready", "lam_sum", "lam_exp", "lam_ready"))
        score_mm, score_read, negmax, exp_ready, prob_ready = (sem(n) for n in ("score_mm", "score_read", "negmax", "exp_ready", "prob_ready"))
        pt_mm, pt_ready, pv_mm, y_ready = (sem(n) for n in ("pt_mm", "pt_ready", "pv_mm", "y_ready"))
        sq_mm, rms_ready, ydiff_ready = sem("sq_mm"), sem("rms_ready"), sem("ydiff_ready")
        out_mm, x2_ready, logit_mm, dve_step = (sem(n) for n in ("out_mm", "x2_ready", "logit_mm", "dve_step"))
        group_sub, group_exp, pair_sub, pair_exp = (sem(n) for n in ("group_sub", "group_exp", "pair_sub", "pair_exp"))
        routed, pos_mm, placed = (sem(n) for n in ("routed", "pos_mm", "placed"))
        hi_ready, lo_ready, split_used = sem("hi_ready"), sem("lo_ready"), sem("split_used")
        onehot_ready, prep_mm, gather_mm, scatT_ready, xt_ready = (
            sem(n) for n in ("onehot_ready", "prep_mm", "gather_mm", "scatT_ready", "xt_ready"))
        gu_read, gt_mm, silu_ready, hid_step, hid_ready = (
            sem(n) for n in ("gu_read", "gt_mm", "silu_ready", "hid_step", "hid_ready"))
        zero_ready, acc_zero, xh_ready, part_ready, rest_ready, h3_ready = (
            sem(n) for n in ("zero_ready", "acc_zero", "xh_ready", "part_ready", "rest_ready", "h3_ready"))
        yh_ready, yl_ready, scat_mm = sem("yh_ready"), sem("yl_ready"), sem("scat_mm")
        cur_ready, pass_shift, final_row, stored = sem("cur_ready"), sem("pass_shift"), sem("final_row"), sem("stored")

        block = ctx.enter_context(nc.Block())

        def by_pairs(eng, pair):
            pair(0)
            with eng.Fori(1, N_EXPERTS // 2) as i:
                pair(i)

        def all_passes(eng, one_pass):
            one_pass(0)
            most = eng.value_load(maxcnt[0:1, 0:1], min_val=0, max_val=SEQ)
            for p in range(1, PASSES):
                with eng.If(most > SLOTS * p):
                    one_pass(p)

        def experts_before(i, odd, p):
            return i * 2 + (odd + N_EXPERTS * p)

        def units_before(i, odd, p, u):
            return i * (2 * UPE) + (UPE * odd + u + N_EXPERTS * UPE * p)

        def turn_in_pass(i, odd):
            return odd if isinstance(i, int) else 2

        def ring_slot(odd, u):
            return slot_of(BASE + UPE * odd + u)

        def unit_source(e, u):
            if u < 4:
                w = (w_gate, w_up)[u // 2]
                v = w.rearrange("l e (h k p) f -> h (l e) p k f", p=P, h=2)[u % 2]
            else:
                v = w_down.rearrange("l e (h k p) f -> h (l e) p k f", p=P, h=2)[u - 4]
            return v[bass.ds(e, 1)].rearrange("a p k f -> p (a k) f")

        @block.sync
        def _(sp):
            def load(n, source):
                k = source.shape[1]
                sp.dma_start(W[slot_of(n)][:].rearrange("p (k f) -> p k f", k=k), source).then_inc(unit_in[slot_of(n)], 16)

            def wait_reader(n):
                kind, a, b = UNITS[n]
                if kind == "ada":
                    sp.wait_ge(ada_used, ADA_ORDER.index(UNITS[n]) + 1)
                elif kind == "win":
                    sp.wait_ge(win_used, a + 1)
                else:
                    sp.wait_ge(out_mm, TT)

            for n, (kind, a, b) in enumerate(UNITS):
                if n >= RING:
                    wait_reader(n - RING)
                if kind == "ada":
                    load(n, w_ada[0, b * P:(b + 1) * P, a * UW:(a + 1) * UW].rearrange("p (k f) -> p k f", k=1))
                elif kind == "win":
                    load(n, w_in[0].rearrange("(h k p) n -> h p k n", h=2, p=P)[b][:, :, a * 512:(a + 1) * 512])
                else:
                    load(n, w_out[0].rearrange("(h k p) n -> h p k n", h=4, p=P)[a])

            def stream(p):
                first = 32 * p * UPE
                for u in range(2 * UPE):
                    if p == 0:
                        wait_reader(BASE + u - RING)
                    else:
                        sp.wait_ge(split_used, first + u + 1 - RING)
                    load(BASE + first + u, unit_source(u // UPE, u % UPE))
                with sp.Fori(1, N_EXPERTS // 2) as i:
                    for u in range(2 * UPE):
                        sp.wait_ge(split_used, i * (2 * UPE) + (first + u + 1 - RING))
                        load(BASE + u, unit_source(i * 2 + u // UPE, u % UPE))

            stream(0)
            sp.wait_ge(placed, 1)
            most = sp.value_load(maxcnt[0:1, 0:1], min_val=0, max_val=SEQ)
            for p in range(1, PASSES):
                with sp.If(most > SLOTS * p):
                    stream(p)
            out_v = out[0].rearrange("(t p) d -> p t d", p=P)
            for t in range(TT):
                sp.wait_ge(final_row, t + 1)
                sp.dma_start(out_v[:, t, :], Hn[:, t, :]).then_inc(stored, 16)
            sp.wait_ge(stored, 16 * TT)

        @block.gpsimd
        def _(pool):
            nc.gpsimd.memset(MOD[:], 0.0).then_inc(mod_zero, 1)
            nc.gpsimd.memset(MODG[:], 0.0).then_inc(mod_zero, 1)
            nc.gpsimd.memset(ones[:], 1.0).then_inc(pool_step, 1)
            nc.gpsimd.memset(epsb[:], EPS).then_inc(consts, 1)
            pool.wait_ge(pool_step, 1)
            nc.gpsimd.affine_select(out=ident[:], in_=ones[:], compare_op=ALU.is_equal, fill=0.0, base=0,
                                    pattern=[[-1, P]], channel_multiplier=1).then_inc(consts, 1)
            nc.gpsimd.affine_select(out=flip[:], in_=ones[:], compare_op=ALU.is_equal, fill=0.0, base=1 - P,
                                    pattern=[[1, P]], channel_multiplier=1).then_inc(consts, 1)
            nc.gpsimd.affine_select(out=before[:], in_=ones[:], compare_op=ALU.is_gt, fill=0.0, base=0,
                                    pattern=[[1, P]], channel_multiplier=-1).then_inc(consts, 1)
            nc.gpsimd.iota(slot_no[:], pattern=[[0, 2], [1, SLOTS]], base=0, channel_multiplier=0,
                           allow_small_or_imprecise_dtypes=True).then_inc(consts, 1)
            nc.gpsimd.iota(num32[:], pattern=[[0, TT], [1, N_EXPERTS]], base=-64, channel_multiplier=0,
                           allow_small_or_imprecise_dtypes=True).then_inc(consts, 1)
            pool.wait_ge(consts, 2)
            nc.gpsimd.tensor_copy(ident16[:], ident[:]).then_inc(consts, 1)
            nc.gpsimd.tensor_tensor(stack2[:], ident[:, 0:SLOTS], ident[:, SLOTS:P], ALU.add).then_inc(consts, 1)
            nc.gpsimd.memset(line[:], NEG).then_inc(pool_step, 1)
            pool.wait_ge(pool_step, 2)
            pool.wait_ge(tab_in, 16)
            spread = buckets()
            for lo, hi, b in spread:
                nc.gpsimd.tensor_scalar(line[:, 255 - hi:256 - lo], ones[0:N_BIAS, 0:1].to_broadcast([N_BIAS, hi - lo + 1]),
                                        tabT[:, b:b + 1], None, ALU.mult).then_inc(table_set, 1)
            pool.wait_ge(table_set, len(spread))
            pool.dma_start(line_dram, line[:]).then_inc(line_out, 16)
            pool.wait_ge(line_out, 16)
            pool.dma_start(toe[:], bass.AP(line_dram.tensor, 0, [[1, P], [3 * P, N_BIAS], [1, SEQ]])).then_inc(toe_in, 16)

            def column(e, buf):
                nc.gpsimd.tensor_copy(cur[:, buf, :, :], PG[:, bass.ds(e, 1), :, :].rearrange("p e a t -> p (e a) t")).then_inc(cur_ready, 1)

            def prepare(e, buf, m, n):
                pool.wait_ge(cur_ready, m)
                if not isinstance(n, int) or n:
                    pool.wait_ge(onehot_ready, n * (2 * TT))
                column(e + 1, 1 - buf)
                for t in range(TT):
                    nc.gpsimd.tensor_scalar(OH[:, buf, t, :], slot_no[:], cur[:, buf, 0, t:t + 1], None,
                                            ALU.is_equal).then_inc(onehot_ready, 1)
                    nc.gpsimd.tensor_scalar(OG[:, buf, t, :], slot_no[:], cur[:, buf, 0, t:t + 1],
                                            cur[:, buf, 1, t:t + 1], ALU.is_equal, ALU.mult).then_inc(onehot_ready, 1)

            def one_pass(p):
                at = (N_EXPERTS + 1) * p
                if p == 0:
                    pool.wait_ge(placed, 1)
                else:
                    pool.wait_ge(pass_shift, p)
                    pool.wait_ge(prep_mm, N_EXPERTS * p)
                    pool.wait_ge(cur_ready, at)
                column(0, 0)
                prepare(0, 0, at + 1, N_EXPERTS * p)
                prepare(1, 1, at + 2, N_EXPERTS * p + 1)
                with pool.Fori(1, N_EXPERTS // 2) as i:
                    for odd in (0, 1):
                        n = experts_before(i, odd, p)
                        pool.wait_ge(prep_mm, n - 1)
                        prepare(i * 2 + odd, odd, i * 2 + (odd + 1 + at), n)

            all_passes(pool, one_pass)

        @block.scalar
        def _(act):
            def broadcast(row, n):
                return bass.AP(row.tensor, row.offset, [[0, P], [1, n]])

            with nc.allow_non_contiguous_dma(reason="small columns"):
                act.dma_start(cT[:], c.rearrange("b (k p) -> p (b k)", p=P)).then_inc(c_in, 16)
                act.dma_start(X[:], x[0].rearrange("(t p) d -> p t d", p=P)).then_inc(x_in, 16)
                act.dma_start(tabT[:], rel_bias.rearrange("b h -> h b")).then_inc(tab_in, 16)
                act.wait_ge(mod_zero, 2)
                act.dma_start(MOD[0:1, :], b_ada[:, 0:5 * D]).then_inc(ada_b_in, 16)
                act.dma_start(MODG[0:1, :], b_ada[:, 5 * D:6 * D]).then_inc(ada_b_in, 16)
                for n, row in enumerate((pre_mix_gain, post_mix_gain, pre_ffn_gain)):
                    act.dma_start(gain[:, n, :], broadcast(row, D)).then_inc(gain_in, 16)
                act.dma_start(G2[:], broadcast(post_ffn_gain, D)).then_inc(gain_in, 16)
                for n, row in enumerate((lambda_q1, lambda_q2, lambda_k1, lambda_k2)):
                    act.dma_start(lams[:, n, :], broadcast(row, HEAD)).then_inc(lam_in, 16)
                act.dma_start(hgain[:], diff_head_gain.rearrange("l d -> d l")).then_inc(hgain_in, 16)
                act.dma_start(wr[:, :, 0:N_GROUPS], w_group[0].rearrange("(k p) n -> p k n", p=P)).then_inc(router_in, 16)
                act.dma_start(wr[:, :, N_GROUPS:], w_expert[0].rearrange("(k p) n -> p k n", p=P)).then_inc(router_in, 16)
                act.dma_start(brow[:, 0:N_GROUPS], b_group).then_inc(router_in, 16)
                act.dma_start(brow[:, N_GROUPS:], b_expert).then_inc(router_in, 16)

            act.wait_ge(c_in, 16)
            nc.scalar.activation(cS[:], cT[:], ACT.Silu).then_inc(c_silu, 1)

            def root_mean(n, source, squares):
                nc.scalar.activation(squares, source, ACT.Square, accum_out=st[:, n:n + 1]).then_inc(stat_sq, 1)
                act.wait_ge(stat_sq, n + 1)
                nc.scalar.activation(st[:, n:n + 1], st[:, n:n + 1], ACT.Sqrt, bias=epsb[:], scale=1.0 / D).then_inc(stat_std, 1)

            act.wait_ge(x_in, 16)
            act.wait_ge(consts, 1)
            for t in range(TT):
                root_mean(t, X[:, t, :], Hn[:, t, :])
            for b in range(6):
                act.wait_ge(toe_mm, b + 1)
                nc.scalar.copy(toe[:, 2 * b:2 * b + 2, :], PS[:, b, :].rearrange("p (h j) -> p h j", h=2)).then_inc(toe_ready, 1)
            act.wait_ge(mod_mm, 1)
            nc.scalar.copy(MOD[:, 0:D], PS[:, 0:2, :].rearrange("p b f -> p (b f)")).then_inc(mod_row, 1)
            for g in range(4):
                act.wait_ge(hT_mm, g + 1)
                nc.scalar.copy(hT[:, 4 * (g % 2):4 * (g % 2) + 4, (g // 2) * P:(g // 2 + 1) * P],
                               PS[:, 4 + g, :].rearrange("p (k t) -> p k t", k=4)).then_inc(hT_ready, 1)
            for b in range(6):
                act.wait_ge(win_used, b + 1)
                two = PS[:, 2 * (b % 2):2 * (b % 2) + 2, :]
                if b in (2, 5):
                    nc.scalar.copy(Hn[:, :, (b // 3) * 512:(b // 3) * 512 + 512], two).then_inc(proj_ready, 1)
                else:
                    chunk = {0: 0, 1: 4, 3: 8, 4: 12}[b]
                    nc.scalar.mul(qkT[:, chunk:chunk + 4, :], two.rearrange("p b (s t) -> p (b s) t", t=SEQ),
                                  HEAD ** -0.5 if b in (0, 3) else 1.0).then_inc(proj_ready, 1)
            act.wait_ge(mod_mm, 2)
            nc.scalar.copy(MOD[:, 3 * D:4 * D], PS[:, 6:8, :].rearrange("p b f -> p (b f)")).then_inc(mod_row, 1)
            act.wait_ge(lam_sum, 1)
            nc.scalar.activation(st[:, 10:12], st[:, 8:10], ACT.Exp).then_inc(lam_exp, 1)

            def exps(g):
                act.wait_ge(negmax, 2 * (g + 1))
                for m in range(2):
                    for t, cols in ((0, slice(0, P)), (1, slice(P, 3 * P))):
                        col = 16 + 8 * (g % 2) + 2 * t + m
                        nc.scalar.activation(S[:, g % 2, m, cols], S[:, g % 2, m, cols], ACT.Exp,
                                             bias=st[:, col:col + 1],
                                             accum_out=st[:, col + 4:col + 5]).then_inc(exp_ready, 1)

            exps(0)
            for g in range(PAIRS):
                if g + 1 < PAIRS:
                    exps(g + 1)
                act.wait_ge(pt_mm, g + 1)
                if g:
                    act.wait_ge(pv_mm, g)
                maps = 1 if g < N_DIFF else 2
                nc.scalar.copy(PT[:, 0:maps, :], PS[:, 4:4 + maps, 0:3 * P]).then_inc(pt_ready, 1)
                act.wait_ge(pv_mm, g + 1)
                nc.scalar.copy(hT[:, g, :], PS[:, 6 + g % 2, 0:SEQ]).then_inc(y_ready, 1)
                if g < N_DIFF:
                    nc.scalar.activation(sq[:, g * SEQ:(g + 1) * SEQ], PS[:, 6 + g % 2, 0:SEQ], ACT.Square).then_inc(y_ready, 1)
            act.wait_ge(sq_mm, 1)
            nc.scalar.activation(rs, PS[:, 0:2, :].rearrange("p b f -> p (b f)"), ACT.Sqrt, bias=epsb[:],
                                 scale=1.0 / (2 * HEAD)).then_inc(rms_ready, 1)
            act.wait_ge(out_mm, TT)
            for t in range(TT):
                root_mean(2 + t, ACC[:, t, :], Hn[:, t, :])
            for t in range(TT):
                act.wait_ge(x2_ready, t + 1)
                root_mean(4 + t, X[:, t, :], Hn[:, t, :])
            for g in range(4):
                act.wait_ge(hT_mm, 4 + g + 1)
                nc.scalar.copy(hT[:, 4 * (g % 2):4 * (g % 2) + 4, (g // 2) * P:(g // 2 + 1) * P],
                               PS[:, g, :].rearrange("p (k t) -> p k t", k=4)).then_inc(hT_ready, 1)
            for part in range(2):
                for t in range(TT):
                    if part:
                        act.wait_ge(rest_ready, t + 1)
                    nc.scalar.copy(H3[:, part, t, :], Hn[:, t, :]).then_inc(part_ready, 1)
            act.wait_ge(group_sub, 1)
            nc.scalar.activation(rt[:, 0, :, 0:N_GROUPS], rt[:, 0, :, 0:N_GROUPS], ACT.Exp).then_inc(group_exp, 1)
            act.wait_ge(pair_sub, 1)
            nc.scalar.activation(st[:, 44:46], st[:, 44:46], ACT.Exp).then_inc(pair_exp, 1)
            act.wait_ge(pos_mm, 1)

            def one_pass(p):
                def split_high(i, odd, u):
                    n = units_before(i, odd, p, u)
                    ready = 16 * uses_of(BASE + UPE * odd + u) + 16 * (N_EXPERTS // 2) * p
                    act.wait_ge(unit_in[ring_slot(odd, u)], i * 16 + ready)
                    if turn_in_pass(i, odd) or u >= SPLITS or p:
                        act.wait_ge(split_used, n + (1 - SPLITS))
                    nc.scalar.copy(WH[:, (UPE * odd + u) % SPLITS, :], W[ring_slot(odd, u)][:]).then_inc(hi_ready, 1)

                def output_high(buf, units):
                    act.wait_ge(split_used, units)
                    nc.scalar.mul(YH[:], PS[:, 2:4, :].rearrange("p b f -> p (b f)"),
                                  gcol[:, buf:buf + 1]).then_inc(yh_ready, 1)

                def tokens(n):
                    act.wait_ge(gather_mm, n + 1)
                    nc.scalar.copy(XT[:, :, 0, :], PS[:, 2, :].rearrange("p (k s) -> p k s", k=DC)).then_inc(xh_ready, 1)

                def gate_up(n):
                    act.wait_ge(split_used, n * UPE + 4)
                    nc.scalar.copy(GU[:], PS[:, 0:2, :].rearrange("p b f -> p (b f)")).then_inc(gu_read, 1)

                def silu(n):
                    act.wait_ge(gt_mm, n + 1)
                    nc.scalar.activation(SG[:], PS[:, 0, 0:FC * SLOTS], ACT.Silu).then_inc(silu_ready, 1)

                def slots(n, buf, used):
                    act.wait_ge(prep_mm, n + 1)
                    if used:
                        act.wait_ge(scat_mm, n - 1)
                    nc.scalar.copy(ST[:, buf, :], PS[:, 1, :].bitcast(bf16)[:, 0:SEQ]).then_inc(scatT_ready, 1)
                    nc.scalar.copy(gcol[:, buf:buf + 1], PS[:, 1, SEQ:SEQ + 1]).then_inc(scatT_ready, 1)

                def pair(i):
                    for odd in (0, 1):
                        n = experts_before(i, odd, p)
                        turn = turn_in_pass(i, odd)
                        split_high(i, odd, 0)
                        if turn:
                            gate_up(n - 1)
                        tokens(n)
                        if turn:
                            silu(n - 1)
                        split_high(i, odd, 1)
                        slots(n, odd, turn == 2 or p)
                        split_high(i, odd, 2)
                        if turn:
                            output_high(1 - odd, units_before(i, odd, p, 0))
                        for u in (3, 4, 5):
                            split_high(i, odd, u)

                by_pairs(act, pair)
                end = N_EXPERTS * (p + 1)
                gate_up(end - 1)
                silu(end - 1)
                output_high(1, UPE * end)
                act.wait_ge(scat_mm, end)

            act.wait_ge(placed, 1)
            all_passes(act, one_pass)
            for t in range(TT):
                root_mean(6 + t, ACC[:, t, :], junk)

        @block.vector
        def _(dve):
            steps = [0]

            def link(ins):
                steps[0] += 1
                ins.then_inc(dve_step, 1)
                dve.wait_ge(dve_step, steps[0])

            def ada(n):
                _, a, k = ADA_ORDER[n]
                at = UNIT_AT[ADA_ORDER[n]]
                dve.wait_ge(unit_in[slot_of(at)], 16 * uses_of(at))
                if n:
                    dve.wait_ge(ada_used, n)
                if a < 2:
                    m = MOD[:, a * UW:(a + 1) * UW]
                    nc.vector.scalar_tensor_tensor(m, W[slot_of(at)][:, :], cS[:, k:k + 1], m,
                                                   ALU.mult, ALU.add).then_inc(ada_used, 1)
                else:
                    link(nc.vector.scalar_tensor_tensor(MOD[:, 4 * D:5 * D], W[slot_of(at)][:, 0:D], cS[:, k:k + 1],
                                                        MOD[:, 4 * D:5 * D], ALU.mult, ALU.add))
                    nc.vector.scalar_tensor_tensor(MODG[:], W[slot_of(at)][:, D:2 * D], cS[:, k:k + 1],
                                                   MODG[:], ALU.mult, ALU.add).then_inc(ada_used, 1)

            dve.wait_ge(c_silu, 1)
            dve.wait_ge(ada_b_in, 32)
            dve.wait_ge(mod_zero, 2)
            for n in range(DC):
                ada(n)

            def inverse(n):
                dve.wait_ge(stat_std, n + 1)
                nc.vector.reciprocal(st[:, 48 + n:49 + n], st[:, n:n + 1]).then_inc(stat_inv, 1)

            def modulate(t, scale, shift, n):
                dve.wait_ge(stat_inv, n + 1)
                link(nc.vector.scalar_tensor_tensor(Hn[:, t, :], X[:, t, :], st[:, 48 + n:49 + n], scale, ALU.mult, ALU.mult))
                nc.vector.tensor_tensor(Hn[:, t, :], Hn[:, t, :], shift, ALU.add).then_inc(h_ready, 1)

            inverse(0)
            inverse(1)
            dve.wait_ge(gain_in, 64)
            dve.wait_ge(mod_mm, 1)
            link(nc.vector.scalar_tensor_tensor(MOD[:, D:2 * D], PS[:, 2:4, :].rearrange("p b f -> p (b f)"), 1.0, gain[:, 0, :],
                                                ALU.add, ALU.mult))
            dve.wait_ge(mod_row, 1)
            for t in range(TT):
                modulate(t, MOD[:, D:2 * D], MOD[:, 0:D], t)

            for n in range(DC, 3 * DC):
                ada(n)

            dve.wait_ge(lam_in, 64)
            link(nc.vector.tensor_tensor(lams[:, 0:2, :], lams[:, 0:2, :], lams[:, 2:4, :], ALU.mult))
            nc.vector.tensor_reduce(st[:, 8:10], lams[:, 0:2, :], AX.X, ALU.add).then_inc(lam_sum, 1)
            dve.wait_ge(lam_exp, 1)
            link(nc.vector.tensor_tensor(st[:, 12:13], st[:, 11:12], st[:, 10:11], ALU.subtract))
            link(nc.vector.tensor_scalar(st[:, 13:14], st[:, 12:13], -LAMBDA_INIT, None, ALU.add))
            dve.wait_ge(hgain_in, 16)
            link(nc.vector.tensor_scalar(hgain[:], hgain[:], 1.0 - LAMBDA_INIT, None, ALU.mult))
            dve.wait_ge(mod_mm, 2)
            nc.vector.tensor_tensor(MOD[:, 2 * D:3 * D], PS[:, 4:6, :].rearrange("p b f -> p (b f)"), gain[:, 1, :],
                                    ALU.mult).then_inc(mod_row, 1)
            dve.wait_ge(mod_mm, 3)
            nc.vector.scalar_tensor_tensor(MOD[:, 4 * D:5 * D], PS[:, 0:2, :].rearrange("p b f -> p (b f)"), 1.0, gain[:, 2, :],
                                           ALU.add, ALU.mult).then_inc(mod_row, 1)
            nc.vector.tensor_tensor(G2[:], PS[:, 2:4, :].rearrange("p b f -> p (b f)"), G2[:], ALU.mult).then_inc(mod_row, 1)

            dve.wait_ge(toe_ready, 6)

            def scores(g):
                if g >= 2:
                    dve.wait_ge(pt_mm, g - 1)
                dve.wait_ge(score_mm, g + 1)
                b = 2 * (g % 2)
                s0 = 16 + 8 * (g % 2)
                for t, cols, j in ((0, slice(0, P), slice(P, 2 * P)), (1, slice(P, 3 * P), slice(0, 2 * P))):
                    if g < N_DIFF:
                        bias = toe[:, g:g + 1, j].to_broadcast([P, 2, j.stop - j.start])
                    else:
                        h = N_DIFF + 2 * (g - N_DIFF)
                        bias = toe[:, h:h + 2, j]
                    nc.vector.tensor_tensor(S[:, g % 2, :, cols], PS[:, b:b + 2, cols], bias, ALU.add).then_inc(score_read, 1)
                for t, cols in ((0, slice(0, P)), (1, slice(P, 3 * P))):
                    dve.wait_ge(score_read, 2 * g + 1 + t)
                    nc.vector.tensor_reduce(st[:, s0 + 2 * t:s0 + 2 * t + 2], S[:, g % 2, :, cols], AX.X, ALU.max,
                                            negate=True).then_inc(negmax, 1)

            def probabilities(g):
                dve.wait_ge(exp_ready, 4 * (g + 1))
                s0 = 16 + 8 * (g % 2)
                inv = 32 + 4 * (g % 2)
                link(nc.vector.reciprocal(st[:, inv:inv + 4], st[:, s0 + 4:s0 + 8]))
                if g < N_DIFF:
                    for t in range(2):
                        link(nc.vector.tensor_tensor(st[:, 40 + t:41 + t], st[:, inv + 2 * t + 1:inv + 2 * t + 2], st[:, 13:14], ALU.mult))
                for t, cols in ((0, slice(0, P)), (1, slice(P, 3 * P))):
                    for m in range(2):
                        e = S[:, g % 2, m, cols]
                        r = st[:, inv + 2 * t + m:inv + 2 * t + m + 1]
                        if g < N_DIFF and m == 1:
                            r = st[:, 40 + t:41 + t]
                        ins = nc.vector.tensor_scalar(e, e, r, None, ALU.mult)
                        if g >= N_DIFF:
                            ins.then_inc(prob_ready, 1)
                        elif m == 1:
                            link(ins)
                    if g < N_DIFF:
                        nc.vector.tensor_tensor(S[:, g % 2, 0, cols], S[:, g % 2, 0, cols], S[:, g % 2, 1, cols],
                                                ALU.add).then_inc(prob_ready, 2)

            scores(0)
            for g in range(PAIRS):
                if g + 1 < PAIRS:
                    scores(g + 1)
                probabilities(g)
            dve.wait_ge(rms_ready, 1)
            link(nc.vector.reciprocal(rs, rs))
            yd = hT[:, 0:N_DIFF, :].rearrange("p h t -> p (h t)")
            nc.vector.scalar_tensor_tensor(yd, yd, hgain[:], rs, ALU.mult, ALU.mult).then_inc(ydiff_ready, 1)
            for t in range(TT):
                inverse(2 + t)
                dve.wait_ge(stat_inv, 3 + t)
                link(nc.vector.scalar_tensor_tensor(Hn[:, t, :], ACC[:, t, :], st[:, 50 + t:51 + t], MOD[:, 2 * D:3 * D],
                                                    ALU.mult, ALU.mult))
                nc.vector.tensor_tensor(X[:, t, :], X[:, t, :], Hn[:, t, :], ALU.add).then_inc(x2_ready, 1)
            for t in range(TT):
                inverse(4 + t)
                modulate(t, MOD[:, 4 * D:5 * D], MOD[:, 3 * D:4 * D], 4 + t)

            for t in range(TT):
                dve.wait_ge(hT_mm, 4 + 2 * (t + 1))
                dve.wait_ge(part_ready, t + 1)
                nc.vector.tensor_tensor(Hn[:, t, :], Hn[:, t, :], H3[:, 0, t, :], ALU.subtract).then_inc(rest_ready, 1)
            for t in range(TT):
                dve.wait_ge(part_ready, TT + t + 1)
                nc.vector.tensor_tensor(H3[:, 2, t, :], Hn[:, t, :], H3[:, 1, t, :], ALU.subtract).then_inc(h3_ready, 1)

            R = [rt[:, k, :, :] for k in range(10)]
            L = logits[:]
            G, E = L[:, :, 0:N_GROUPS], L[:, :, N_GROUPS:]
            g4 = lambda k: rt[:, k, :, 0:N_GROUPS]

            def spread(v, n):
                return v.rearrange("p (t o) -> p t o", o=1).to_broadcast([P, TT, n])

            def first_of(vals, most, k, n):
                a, b = rt[:, k, :, 0:n], rt[:, k + 1, :, 0:n]
                link(nc.vector.tensor_tensor(a, vals, spread(most, n), ALU.is_equal))
                link(nc.vector.tensor_tensor(b, a, num32[:, :, 0:n], ALU.mult))
                link(nc.vector.tensor_reduce(st[:, 46:48], b, AX.X, ALU.min))
                link(nc.vector.tensor_tensor(a, num32[:, :, 0:n], spread(st[:, 46:48], n), ALU.is_equal))
                return a

            dve.wait_ge(logit_mm, 1)
            link(nc.vector.tensor_copy(L, PS[:, 0, 0:TT * 36].rearrange("p (t n) -> p t n", t=TT)))
            gm, gw, m1, m2, d, t1 = (st[:, a:a + 2] for a in (32, 34, 36, 38, 44, 40))
            link(nc.vector.tensor_reduce(gm, G, AX.X, ALU.max))
            nc.vector.tensor_tensor(g4(0), G, spread(gm, N_GROUPS), ALU.subtract).then_inc(group_sub, 1)
            gsel = first_of(G, gm, 1, N_GROUPS)
            link(nc.vector.tensor_scalar(g4(3), gsel, -1.0, -NEG, ALU.add, ALU.mult))
            link(nc.vector.tensor_tensor(R[4].rearrange("p t (g j) -> p t g j", g=N_GROUPS),
                                         E.rearrange("p t (g j) -> p t g j", g=N_GROUPS),
                                         g4(3).rearrange("p t (g o) -> p t g o", o=1).to_broadcast([P, TT, N_GROUPS, PER_GROUP]),
                                         ALU.add))
            link(nc.vector.tensor_reduce(m1, R[4], AX.X, ALU.max))
            o1 = first_of(R[4], m1, 5, N_EXPERTS)
            link(nc.vector.scalar_tensor_tensor(R[7], o1, 3.0 * NEG, R[4], ALU.mult, ALU.add))
            link(nc.vector.tensor_reduce(m2, R[7], AX.X, ALU.max))
            nc.vector.tensor_tensor(d, m2, m1, ALU.subtract).then_inc(pair_sub, 1)
            o2 = first_of(R[7], m2, 8, N_EXPERTS)
            dve.wait_ge(group_exp, 1)
            link(nc.vector.tensor_reduce(gw, g4(0), AX.X, ALU.add))
            link(nc.vector.reciprocal(gw, gw))
            dve.wait_ge(pair_exp, 1)
            link(nc.vector.tensor_scalar(t1, d, 1.0, None, ALU.add))
            link(nc.vector.reciprocal(t1, t1))
            link(nc.vector.tensor_tensor(t1, t1, gw, ALU.mult))
            link(nc.vector.tensor_tensor(d, d, t1, ALU.mult))
            link(nc.vector.tensor_tensor(R[6], o1, spread(t1, N_EXPERTS), ALU.mult))
            link(nc.vector.tensor_tensor(R[9], o2, spread(d, N_EXPERTS), ALU.mult))
            link(nc.vector.memset(PG[:], -1.0))
            link(nc.vector.memset(PG[:, :, 1, :], 0.0))
            link(nc.vector.tensor_tensor(gates[:, :, 0:N_EXPERTS], R[6], R[9], ALU.add))
            nc.vector.tensor_tensor(R[0], o1, o2, ALU.add).then_inc(routed, 1)
            dve.wait_ge(routed, 1)
            dve.wait_ge(pos_mm, 1)
            place = PS[:, 1, 0:TT * N_EXPERTS].rearrange("p (t n) -> p t n", t=TT)
            link(nc.vector.scalar_tensor_tensor(R[1], place, 1.0, R[0], ALU.add, ALU.mult))
            link(nc.vector.tensor_scalar(posm[:, :, 0:N_EXPERTS], R[1], -1.0, None, ALU.add))
            nc.vector.tensor_reduce(maxcnt[:], PS[0:1, 1, 64:64 + N_EXPERTS], AX.X, ALU.max).then_inc(placed, 1)
            nc.vector.memset(GU[:, 0:512], 0.0).then_inc(zero_ready, 1)

            def one_pass(p):
                if p:
                    dve.wait_ge(onehot_ready, 2 * TT * N_EXPERTS * p)
                    nc.vector.tensor_scalar(PG[:, :, 0, :], PG[:, :, 0, :], -float(SLOTS), None, ALU.add).then_inc(pass_shift, 1)

                def split_low(i, odd, u):
                    n = units_before(i, odd, p, u)
                    dve.wait_ge(hi_ready, n + 1)
                    nc.vector.tensor_tensor(WL[ring_slot(odd, u)][:], W[ring_slot(odd, u)][:],
                                            WH[:, (UPE * odd + u) % SPLITS, :].bitcast(f32), ALU.subtract).then_inc(lo_ready, 1)

                def output_low(buf, done):
                    dve.wait_ge(yh_ready, done)
                    nc.vector.scalar_tensor_tensor(YL[:], PS[:, 2:4, :].rearrange("p b f -> p (b f)"), gcol[:, buf:buf + 1],
                                                   YH[:].bitcast(f32), ALU.mult, ALU.subtract).then_inc(yl_ready, 1)

                def tokens_low(n):
                    dve.wait_ge(xh_ready, n + 1)
                    nc.vector.tensor_tensor(XT[:, :, 1, :], PS[:, 2, :].rearrange("p (k s) -> p k s", k=DC),
                                            XT[:, :, 0, :].bitcast(f32), ALU.subtract).then_inc(xt_ready, 1)

                def hidden(n):
                    whole = HID[:].rearrange("p k s -> p (k s)")
                    dve.wait_ge(silu_ready, n + 1)
                    nc.vector.tensor_tensor(HT[:, :, 0, :], SG[:].rearrange("p (k s) -> p k s", k=FC),
                                            PS[:, 0, FC * SLOTS:].rearrange("p (k s) -> p k s", k=FC), ALU.mult).then_inc(hid_step, 1)
                    nc.vector.tensor_tensor(whole, SG[:], PS[:, 0, FC * SLOTS:], ALU.mult).then_inc(hid_step, 1)
                    dve.wait_ge(hid_step, n * 2 + 2)
                    nc.vector.tensor_tensor(HT[:, :, 1, :], HID[:], HT[:, :, 0, :].bitcast(f32), ALU.subtract).then_inc(hid_ready, 1)

                def pair(i):
                    for odd in (0, 1):
                        n = experts_before(i, odd, p)
                        turn = turn_in_pass(i, odd)
                        tokens_low(n)
                        if turn:
                            hidden(n - 1)
                        for u in (0, 1, 2):
                            split_low(i, odd, u)
                        if turn:
                            output_low(1 - odd, n)
                        for u in (3, 4, 5):
                            split_low(i, odd, u)

                by_pairs(dve, pair)
                hidden(N_EXPERTS * (p + 1) - 1)
                output_low(1, N_EXPERTS * (p + 1))
                dve.wait_ge(scat_mm, N_EXPERTS * (p + 1))

            all_passes(dve, one_pass)
            for t in range(TT):
                inverse(6 + t)
                dve.wait_ge(stat_inv, 7 + t)
                link(nc.vector.scalar_tensor_tensor(Hn[:, t, :], ACC[:, t, :], st[:, 54 + t:55 + t], G2[:], ALU.mult, ALU.mult))
                nc.vector.tensor_tensor(Hn[:, t, :], Hn[:, t, :], X[:, t, :], ALU.add).then_inc(final_row, 1)

        @block.tensor
        def _(pe):
            def arrived(unit):
                at = UNIT_AT[unit]
                pe.wait_ge(unit_in[slot_of(at)], 16 * uses_of(at))

            pe.wait_ge(consts, 8)
            pe.wait_ge(toe_in, 16)
            for b in range(6):
                nc.tensor.matmul(PS[:, b, :], flip[:], toe[:, 2 * b:2 * b + 2, :].rearrange("p h j -> p (h j)"),
                                 start=True, stop=True).then_inc(toe_mm, 1)

            def sum_rows(parts, first_bank):
                for b, part in enumerate(parts):
                    last = nc.tensor.matmul(PS[:, first_bank + b, :], ones[:], part, start=True, stop=True)
                last.then_inc(mod_mm, 1)

            def mod_parts(a):
                return [MOD[:, a * D + 512 * b:a * D + 512 * b + 512] for b in range(2)]

            pe.wait_ge(ada_used, DC)
            pe.wait_ge(toe_ready, 6)
            sum_rows(mod_parts(0) + mod_parts(1), 0)

            def transpose_h(first_h, bank):
                for t in range(TT):
                    pe.wait_ge(h_ready, first_h + t + 1)
                    for half in range(2):
                        for k in range(4):
                            last = nc.tensor.transpose(PS[:, bank + 2 * t + half, k * P:(k + 1) * P],
                                                       Hn[:, t, (4 * half + k) * P:(4 * half + k + 1) * P], ident[:])
                        last.then_inc(hT_mm, 1)

            transpose_h(0, 4)
            pe.wait_ge(hT_ready, 4)
            for b in range(6):
                arrived(("win", b, 0))
                arrived(("win", b, 1))
                if b >= 2:
                    pe.wait_ge(proj_ready, b - 1)
                w = [W[slot_of(UNIT_AT["win", b, k // 4])][:, (k % 4) * 512:(k % 4 + 1) * 512] for k in range(DC)]
                bank = 2 * (b % 2)
                if b in (2, 5):
                    for t in range(TT):
                        for k in range(DC):
                            last = nc.tensor.matmul(PS[:, bank + t, :], hT[:, k, t * P:(t + 1) * P], w[k],
                                                    start=(k == 0), stop=(k == DC - 1))
                else:
                    for s in range(4):
                        for k in range(DC):
                            last = nc.tensor.matmul(PS[:, bank + s // 2, (s % 2) * SEQ:(s % 2 + 1) * SEQ],
                                                    w[k][:, s * P:(s + 1) * P], hT[:, k, :],
                                                    start=(k == 0), stop=(k == DC - 1))
                last.then_inc(win_used, 1)
            pe.wait_ge(ada_used, 3 * DC)
            sum_rows(mod_parts(2) + mod_parts(3), 4)
            pe.wait_ge(proj_ready, 6)
            sum_rows(mod_parts(4) + [MODG[:, 0:512], MODG[:, 512:1024]], 0)

            def score(g):
                if g < N_DIFF:
                    q, k = g, 4 + g
                else:
                    q, k = 8 + g - N_DIFF, 12 + g - N_DIFF
                if g == 0:
                    pe.wait_ge(mod_row, 5)
                if g >= 2:
                    pe.wait_ge(score_read, 2 * (g - 1))
                for t in range(TT):
                    for m in range(2):
                        half = slice(64 * m, 64 * m + 64)
                        last = nc.tensor.matmul(PS[:, 2 * (g % 2) + m, (0 if t == 0 else P):(P if t == 0 else 3 * P)],
                                                qkT[half, q, t * P:(t + 1) * P], qkT[half, k, 0:(t + 1) * P],
                                                start=True, stop=True)
                last.then_inc(score_mm, 1)

            def transpose_probabilities(g):
                pe.wait_ge(prob_ready, 4 * (g + 1))
                if g:
                    pe.wait_ge(pt_ready, g)
                for m in range(1 if g < N_DIFF else 2):
                    for n in range(3):
                        last = nc.tensor.transpose(PS[:, 4 + m, n * P:(n + 1) * P], S[:, g % 2, m, n * P:(n + 1) * P], ident[:])
                last.then_inc(pt_mm, 1)

            def weigh_values(g):
                pe.wait_ge(pt_ready, g + 1)
                if g >= 2:
                    pe.wait_ge(y_ready, 2 * (g - 1) if g - 2 < N_DIFF else 2 * N_DIFF + g - 1 - N_DIFF)
                bank = 6 + g % 2
                if g < N_DIFF:
                    jobs = [(0, slice(0, P), Hn[:, 0, g * P:(g + 1) * P], Hn[:, 1, g * P:(g + 1) * P])]
                else:
                    jobs = []
                    for m in range(2):
                        c0 = 512 + (2 * (g - N_DIFF) + m) * HEAD
                        jobs.append((m, slice(64 * m, 64 * m + 64), Hn[:, 0, c0:c0 + HEAD], Hn[:, 1, c0:c0 + HEAD]))
                for m, rows, v0, v1 in jobs:
                    nc.tensor.matmul(PS[rows, bank, 0:SEQ], v0, PT[:, m, 0:SEQ], start=True, stop=False)
                    last = nc.tensor.matmul(PS[rows, bank, P:SEQ], v1, PT[:, m, SEQ:3 * P], start=False, stop=True)
                last.then_inc(pv_mm, 1)

            score(0)
            score(1)
            for g in range(PAIRS):
                transpose_probabilities(g)
                if g + 2 < PAIRS:
                    score(g + 2)
                weigh_values(g)
            pe.wait_ge(y_ready, 2 * N_DIFF + PAIRS - N_DIFF)
            pe.wait_ge(score_read, 2 * PAIRS)
            for b in range(2):
                last = nc.tensor.matmul(PS[:, b, :], ones[:], sq[:, 512 * b:512 * b + 512], start=True, stop=True)
            last.then_inc(sq_mm, 1)
            order = [4, 5, 6, 7, 0, 1, 2, 3]
            for k in order:
                if k == 4:
                    arrived(("wout", 2, 0))
                if k == 6:
                    arrived(("wout", 3, 0))
                if k == 0:
                    pe.wait_ge(ydiff_ready, 1)
                    arrived(("wout", 0, 0))
                if k == 2:
                    arrived(("wout", 1, 0))
                for t in range(TT):
                    for half in range(2):
                        wo = W[slot_of(UNIT_AT["wout", k // 2, 0])][:, (k % 2) * D + half * 512:(k % 2) * D + half * 512 + 512]
                        last = nc.tensor.matmul(PS[:, 4 + 2 * t + half, :], hT[:, k, t * P:(t + 1) * P], wo,
                                                start=(k == order[0]), stop=(k == order[-1]))
            last.then_inc(out_mm, TT)
            transpose_h(2, 0)
            pe.wait_ge(hT_ready, 8)
            pe.wait_ge(router_in, 64)
            for t in range(TT):
                lg = PS[:, 0, t * 36:(t + 1) * 36]
                for k in range(DC):
                    nc.tensor.matmul(lg, hT[:, k, t * P:(t + 1) * P], wr[:, k, :], start=(k == 0), stop=False)
                last = nc.tensor.matmul(lg, ones[0:1, :], brow[0:1, :], start=False, stop=True)
            last.then_inc(logit_mm, 1)
            pe.wait_ge(routed, 1)
            m0, m1 = rt[:, 0, 0, :], rt[:, 0, 1, :]
            E = N_EXPERTS
            nc.tensor.matmul(PS[:, 1, 0:E], before[:], m0, start=True, stop=True)
            nc.tensor.matmul(PS[:, 1, E:2 * E], ones[:], m0, start=True, stop=False)
            nc.tensor.matmul(PS[:, 1, E:2 * E], before[:], m1, start=False, stop=True)
            nc.tensor.matmul(PS[:, 1, 2 * E:3 * E], ones[:], m0, start=True, stop=False)
            nc.tensor.matmul(PS[:, 1, 2 * E:3 * E], ones[:], m1, start=False, stop=True).then_inc(pos_mm, 1)
            pe.wait_ge(placed, 1)
            pe.wait_ge(zero_ready, 1)
            for b in range(4):
                last = nc.tensor.matmul(PS[:, 4 + b, :], ones[:], GU[:, 0:512], start=True, stop=True)
            last.then_inc(acc_zero, 1)

            pe.wait_ge(h3_ready, TT)
            def one_pass(p):
                def gather(n, buf, turn):
                    pe.wait_ge(onehot_ready, (n + 1) * (2 * TT))
                    if turn == 2 or p:
                        pe.wait_ge(yl_ready, n - 1)
                    for k in range(DC):
                        for t in range(TT):
                            for part in range(3):
                                last = nc.tensor.matmul(PS[:, 2, k * SLOTS:(k + 1) * SLOTS], H3[:, part, t, k * P:(k + 1) * P],
                                                        OH[:, buf, t, 0:SLOTS], start=(t == 0 and part == 0),
                                                        stop=(t == TT - 1 and part == 2))
                    last.then_inc(gather_mm, 1)

                def transpose_gate_up(n):
                    pe.wait_ge(gu_read, n + 1)
                    for q in range(2 * FC):
                        last = nc.tensor.matmul(PS[:, 0, q * SLOTS:(q + 1) * SLOTS], GU[:, q * P:(q + 1) * P], stack2[:],
                                                start=True, stop=True)
                    last.then_inc(gt_mm, 1)

                def prepare(buf):
                    for t in range(TT):
                        nc.tensor.transpose(PS[:, 1, :].bitcast(bf16)[:, t * P:(t + 1) * P], OH[:, buf, t, :], ident16[:])
                    for t in range(TT):
                        last = nc.tensor.matmul(PS[:, 1, SEQ:SEQ + 1], OG[:, buf, t, :], ones[:, 0:1],
                                                start=(t == 0), stop=(t == TT - 1))
                    last.then_inc(prep_mm, 1)

                def scatter(n, buf):
                    pe.wait_ge(yl_ready, n + 1)
                    for t in range(TT):
                        for half in range(2):
                            for y in (YH, YL):
                                last = nc.tensor.matmul(PS[:, 4 + 2 * t + half, :], ST[:, buf, t * P:(t + 1) * P],
                                                        y[:, half * 512:half * 512 + 512],
                                                        start=False, stop=True, skip_group_check=True)
                    last.then_inc(scat_mm, 1)

                def unit(n, at, outs):
                    for high in (True, False):
                        pe.wait_ge(hi_ready if high else lo_ready, n + 1)
                        w = WH[:, at % SPLITS, :] if high else WL[ring_slot(0, at)][:]
                        for q in range(4):
                            bank, lhsT, begin, end = outs(q, high)
                            last = nc.tensor.matmul(PS[:, bank, :], lhsT, w[:, q * 512:(q + 1) * 512],
                                                    start=begin, stop=end)
                    last.then_inc(split_used, 1)

                def gate_up(n, odd):
                    pe.wait_ge(xt_ready, n + 1)
                    pe.wait_ge(scatT_ready, n * 2 + 2)
                    for u in range(4):
                        def into(q, high):
                            k = 4 * (u % 2) + q
                            return (u // 2, XT[:, k, :, :].rearrange("p a s -> p (a s)"),
                                    k == 0 and high, k == DC - 1 and not high)
                        unit(n * UPE + u, UPE * odd + u, into)

                def down(n, odd):
                    pe.wait_ge(hid_ready, n + 1)
                    for u in (4, 5):
                        def into(q, high):
                            k = 2 * (u - 4) + q // 2
                            return (2 + q % 2, HT[:, k, :, :].rearrange("p a s -> p (a s)"),
                                    k == 0 and high, k == FC - 1 and not high)
                        unit(n * UPE + u, UPE * odd + u, into)

                def pair(i):
                    for odd in (0, 1):
                        n = experts_before(i, odd, p)
                        turn = turn_in_pass(i, odd)
                        gather(n, odd, turn)
                        if turn:
                            transpose_gate_up(n - 1)
                        prepare(odd)
                        if turn == 2:
                            scatter(n - 2, odd)
                        if turn:
                            pe.wait_ge(xt_ready, n + 1)
                            down(n - 1, 1 - odd)
                        gate_up(n, odd)

                by_pairs(pe, pair)
                end = N_EXPERTS * (p + 1)
                transpose_gate_up(end - 1)
                scatter(end - 2, 0)
                down(end - 1, 1)
                scatter(end - 1, 1)

            all_passes(pe, one_pass)


_INS = ["x", "c", "w_ada", "b_ada", "pre_mix_gain", "post_mix_gain", "pre_ffn_gain", "post_ffn_gain", "w_in",
        "lambda_q1", "lambda_k1", "lambda_q2", "lambda_k2", "diff_head_gain", "w_out", "rel_bias",
        "w_group", "b_group", "w_expert", "b_expert", "w_gate", "w_up", "w_down"]
_OUT = ((1, 256, 1024), "float32")


def kernel(**inputs):
    import numpy as _np
    import concourse.bacc as _bacc
    from concourse import mybir as _mybir
    from concourse.bass_utils import run_bass_kernel_spmd as _run

    nc = _bacc.Bacc("TRN2", target_bir_lowering=False, num_devices=1)
    arrays, args = {}, []
    for name in _INS:
        a = _np.ascontiguousarray(inputs[name])
        arrays[f"in_{name}_dram"] = a
        args.append(nc.dram_tensor(f"in_{name}_dram", a.shape, _mybir.dt.from_np(a.dtype), kind="ExternalInput").ap())
    args.append(nc.dram_tensor("out_0_dram", _OUT[0], _mybir.dt.from_np(_np.dtype(_OUT[1])), kind="ExternalOutput").ap())
    build(nc, *args)
    r = _run(nc, [arrays], core_ids=[0])
    return r.results[0]["out_0_dram"]
```

```python
import math
from contextlib import ExitStack

import concourse.bass as bass
from concourse import mybir

P = 128
SEQ, D = 256, 1024
TT = SEQ // P
DC = D // P
HEAD = 64
N_DIFF, N_MOBA = 4, 8
N_BIAS = N_DIFF + N_MOBA
PAIRS = N_DIFF + N_MOBA // 2
N_BUCKETS, MAX_DISTANCE = 32, 128
N_GROUPS, PER_GROUP = 4, 8
N_EXPERTS = N_GROUPS * PER_GROUP
FF = D // 2
FC = FF // P
EPS, NEG = 1e-6, -1e30
LAMBDA_INIT = 0.8 - 0.6 * math.exp(-0.3 * 0)

UW = 2048
RING = 12
AHEAD = 2
UPE = 6
SPLITS = 4
SLOTS = 64
PASSES = SEQ // SLOTS
LAST_PAIR = N_EXPERTS // 2 - 1
SPARE = UPE + 3


def prologue_units():
    units = [("ada", 0, k) for k in range(DC)]
    ada2 = [("ada", a, k) for a in (1, 2) for k in range(DC)]
    for b in range(6):
        units += [("win", b, 0), ("win", b, 1)]
        n = 3 if b < 4 else 2
        units += ada2[:n]
        ada2 = ada2[n:]
    return units + [("wout", u, 0) for u in range(4)]


UNITS = prologue_units()
BASE = len(UNITS)
UNIT_AT = {u: n for n, u in enumerate(UNITS)}


def on_tensor(unit):
    return unit[0] == "ada" and unit[1] == 0 and unit[2] % 2 == 1


ADA_ORDER = [u for u in UNITS if u[0] == "ada" and not on_tensor(u)]
FIRST_ADA = DC // 2


def slot_of(n):
    return n % RING


def uses_of(n):
    return n // RING + 1


def buckets():
    exact = N_BUCKETS // 2

    def bucket(d):
        if d < exact:
            return d
        return min(exact + int(math.log(d / exact) / math.log(MAX_DISTANCE / exact) * (N_BUCKETS - exact)),
                   N_BUCKETS - 1)

    out = []
    for d in range(SEQ):
        if out and out[-1][2] == bucket(d):
            out[-1][1] = d
        else:
            out.append([d, d, bucket(d)])
    return out


def build(nc, x, c, w_ada, b_ada, pre_mix_gain, post_mix_gain, pre_ffn_gain, post_ffn_gain, w_in,
          lambda_q1, lambda_k1, lambda_q2, lambda_k2, diff_head_gain, w_out, rel_bias,
          w_group, b_group, w_expert, b_expert, w_gate, w_up, w_down, out):
    f32, f32r, bf16, i32 = mybir.dt.float32, mybir.dt.float32r, mybir.dt.bfloat16, mybir.dt.int32
    ALU, ACT, AX = mybir.AluOpType, mybir.ActivationFunctionType, mybir.AxisListType

    ctx = ExitStack()
    with ctx:
        def sb(name, shape, dt=f32, at=ctx):
            return at.enter_context(nc.sbuf_tensor(name, shape, dt))

        def sem(name):
            return ctx.enter_context(nc.semaphore(name))

        W, WL = [], []
        for slot in range(RING):
            with nc.sbuf_tensor(f"W{slot}", [P, UW], f32) as w:
                W.append(w)
            WL.append(sb(f"WL{slot}", [P, UW], f32r))
        X = sb("X", [P, TT, D])
        with nc.sbuf_tensor("Hn", [P, TT, D], f32) as h:
            Hn = h
        HnL = sb("HnL", [P, UW], f32r)
        G2 = sb("G2", [P, D])
        ident = sb("ident", [P, P])
        ones = sb("ones", [P, P])
        ident16 = sb("ident16", [P, P], bf16)
        stack2 = sb("stack2", [P, SLOTS])
        before = sb("before", [P, P])
        slot_no = sb("slot_no", [P, 2 * SLOTS])
        num32 = sb("num32", [P, TT, N_EXPERTS])
        cT = sb("cT", [P, DC])
        cS = sb("cS", [P, DC])
        st = sb("st", [P, 64])
        epsb = sb("epsb", [P, 1])
        hgain = sb("hgain", [P, 1])
        wr = sb("wr", [P, DC, N_GROUPS + N_EXPERTS])
        brow = sb("brow", [1, N_GROUPS + N_EXPERTS])
        LE = N_EXPERTS + 1
        PG = sb("PG", [P, LE, 2, TT])
        posm = PG[:, :, 0, :].rearrange("p e t -> p t e")
        gates = PG[:, :, 1, :].rearrange("p e t -> p t e")
        cur = sb("cur", [P, 2, 2, TT])
        maxcnt = sb("maxcnt", [1, 1], i32)
        rt = sb("rt", [P, 10, TT, N_EXPERTS])
        logits = sb("logits", [P, TT, N_GROUPS + N_EXPERTS])

        early = ExitStack()
        toe = sb("toe", [P, N_BIAS, SEQ], at=early)
        S = sb("S", [P, 2, 2, 3 * P], at=early)
        PT = sb("PT", [P, 2, 3 * P], at=early)
        tabT = sb("tabT", [N_BIAS, N_BUCKETS], at=early)
        line = sb("line", [N_BIAS, 3 * P], at=early)
        flip = sb("flip", [P, P], at=early)
        gain = sb("gain", [P, 3, D], at=early)
        qkT = sb("qkT", [P, 16, SEQ], at=early)
        hT = sb("hT", [P, DC, SEQ], at=early)
        MOD = sb("MOD", [P, 6 * D], at=early)
        cSb = PT[:].rearrange("p m n -> p (m n)")[:, 256:768].rearrange("p (k m) -> p k m", m=P)
        lams = PT[:, 0, 0:4 * HEAD].rearrange("p (n d) -> p n d", n=4)
        early.close()
        sq = MOD[:, 0:D]
        diag = MOD[:, D:2 * D].rearrange("p (n q) -> p n q", n=N_DIFF * TT)

        WH = sb("WH", [P, SPLITS, UW], f32r)
        H3 = sb("H3", [P, 3, TT, D], bf16)
        GU = sb("GU", [P, 2 * FF])
        XT = sb("XT", [P, DC, 2, SLOTS], f32r)
        SG = sb("SG", [P, FC * SLOTS])
        HID = sb("HID", [P, FC, SLOTS])
        HT = sb("HT", [P, FC, 2, SLOTS], f32r)
        YH = sb("YH", [P, D], f32r)
        YL = sb("YL", [P, D], f32r)
        OH = sb("OH", [P, 2, TT, 2 * SLOTS], bf16)
        OG = sb("OG", [P, 2, TT, 2 * SLOTS])
        ST = sb("ST", [P, 2, SEQ], f32r)
        gcol = sb("gcol", [P, 2])
        junk = W[0][:, 0:D]

        PS = ctx.enter_context(nc.psum_tensor("PS", [P, 8, 512], f32))
        OUT = PS[:, 0:4, :].rearrange("p (t n) f -> p t (n f)", t=TT)
        ACC = PS[:, 4:8, :].rearrange("p (t n) f -> p t (n f)", t=TT)

        line_dram = nc.dram_tensor("line_dram", [N_BIAS, 3 * P], f32).ap()

        unit_in = [sem(f"unit_in{s}") for s in range(RING)]
        spare_in = sem("spare_in")
        ada_used, ada_mm, win_used, cs_ready = sem("ada_used"), sem("ada_mm"), sem("win_used"), sem("cs_ready")
        c_in, x_in, ada_b_in, ada_b_rest, pre_gain_in, gain_in, tab_in, lam_in = (
            sem(n) for n in ("c_in", "x_in", "ada_b_in", "ada_b_rest", "pre_gain_in", "gain_in", "tab_in", "lam_in"))
        router_in, hgain_in, line_out, toe_in = (sem(n) for n in ("router_in", "hgain_in", "line_out", "toe_in"))
        mod_zero, rest_zero, consts, table_set, pool_step = (sem(n) for n in ("mod_zero", "rest_zero", "consts", "table_set", "pool_step"))
        c_silu, toe_mm, toe_ready, mod_mm, mod_row = (sem(n) for n in ("c_silu", "toe_mm", "toe_ready", "mod_mm", "mod_row"))
        stat_sq, stat_std, stat_inv = sem("stat_sq"), sem("stat_std"), sem("stat_inv")
        h_ready, hT_mm, hT_ready = sem("h_ready"), sem("hT_mm"), sem("hT_ready")
        proj_ready, lam_sum, lam_exp = (sem(n) for n in ("proj_ready", "lam_sum", "lam_exp"))
        score_mm, score_read, negmax, exp_ready, prob_ready = (sem(n) for n in ("score_mm", "score_read", "negmax", "exp_ready", "prob_ready"))
        pt_mm, pt_ready, pv_mm, y_ready = (sem(n) for n in ("pt_mm", "pt_ready", "pv_mm", "y_ready"))
        sq_mm, rms_ready, inv_rms, diag_ready, rms_mm, ydiff_ready = (
            sem(n) for n in ("sq_mm", "rms_ready", "inv_rms", "diag_ready", "rms_mm", "ydiff_ready"))
        out_mm, x2_ready, logit_mm, dve_step = (sem(n) for n in ("out_mm", "x2_ready", "logit_mm", "dve_step"))
        group_sub, group_exp, pair_sub, pair_exp = (sem(n) for n in ("group_sub", "group_exp", "pair_sub", "pair_exp"))
        routed, pos_mm, placed = (sem(n) for n in ("routed", "pos_mm", "placed"))
        hi_ready, lo_ready, split_used = sem("hi_ready"), sem("lo_ready"), sem("split_used")
        onehot_ready, prep_mm, gather_mm, scatT_ready, xt_ready = (
            sem(n) for n in ("onehot_ready", "prep_mm", "gather_mm", "scatT_ready", "xt_ready"))
        gu_read, gt_mm, silu_ready, hid_step, hid_ready = (
            sem(n) for n in ("gu_read", "gt_mm", "silu_ready", "hid_step", "hid_ready"))
        zero_ready, xh_ready, part_ready, rest_ready, h3_ready = (
            sem(n) for n in ("zero_ready", "xh_ready", "part_ready", "rest_ready", "h3_ready"))
        yh_ready, yl_ready, scat_mm = sem("yh_ready"), sem("yl_ready"), sem("scat_mm")
        cur_ready, pass_shift, final_row, stored = sem("cur_ready"), sem("pass_shift"), sem("final_row"), sem("stored")
        gained, warm = sem("gained"), sem("warm")

        block = ctx.enter_context(nc.Block())

        def projection_bank(b, half):
            return 2 * (b % 2) + half if b < 3 else half

        def value_bank(g):
            return 6 + g % 2 if g < N_DIFF else 6

        def output_chunk(g):
            return g if g < N_DIFF else 4 + g

        def by_pairs(eng, pair):
            pair(0)
            with eng.Fori(1, LAST_PAIR) as i:
                pair(i)
            pair(LAST_PAIR)

        def all_passes(eng, one_pass):
            one_pass(0)
            most = eng.value_load(maxcnt[0:1, 0:1], min_val=0, max_val=SEQ)
            for p in range(1, PASSES):
                with eng.If(most > SLOTS * p):
                    one_pass(p)

        def experts_before(i, odd, p):
            return i * 2 + (odd + N_EXPERTS * p)

        def units_before(i, odd, p, u):
            return i * (2 * UPE) + (UPE * odd + u + N_EXPERTS * UPE * p)

        def turn_in_pass(i, odd):
            return odd if isinstance(i, int) and i == 0 else 2

        def ahead(i, odd, u, p):
            return isinstance(i, int) and i == 0 and odd == 0 and u < SPLITS and p == 0

        def is_last(i, odd):
            return isinstance(i, int) and i == LAST_PAIR and odd == 1

        def ring_slot(odd, u):
            return slot_of(BASE + UPE * odd + u)

        def is_spare(i, odd, u, p):
            return p == 0 and isinstance(i, int) and i == 0 and UPE * odd + u == SPARE

        def unit_arrived(eng, i, odd, u, p):
            if is_spare(i, odd, u, p):
                eng.wait_ge(spare_in, 16)
                return
            fills = uses_of(BASE + UPE * odd + u) + (N_EXPERTS // 2) * p - (UPE * odd + u == SPARE)
            eng.wait_ge(unit_in[ring_slot(odd, u)], i * 16 + 16 * fills)

        def unit_source(e, u):
            if u < 4:
                w = (w_gate, w_up)[u // 2]
                v = w.rearrange("l e (h k p) f -> h (l e) p k f", p=P, h=2)[u % 2]
            else:
                v = w_down.rearrange("l e (h k p) f -> h (l e) p k f", p=P, h=2)[u - 4]
            return v[bass.ds(e, 1)].rearrange("a p k f -> p (a k) f")

        @block.sync
        def _(sp):
            def load(n, source):
                k = source.shape[1]
                sp.dma_start(W[slot_of(n)][:].rearrange("p (k f) -> p k f", k=k), source).then_inc(unit_in[slot_of(n)], 16)

            def wait_reader(n):
                kind, a, b = UNITS[n]
                if on_tensor(UNITS[n]):
                    sp.wait_ge(ada_mm, b // 2 + 1)
                elif kind == "ada":
                    sp.wait_ge(ada_used, ADA_ORDER.index(UNITS[n]) + 1)
                elif kind == "win":
                    sp.wait_ge(win_used, 2 * (a + 1))
                else:
                    sp.wait_ge(out_mm, TT)

            for n, (kind, a, b) in enumerate(UNITS):
                if n >= RING:
                    wait_reader(n - RING)
                elif n >= AHEAD:
                    sp.wait_ge(unit_in[n - AHEAD], 16)
                if kind == "ada":
                    load(n, w_ada[0, b * P:(b + 1) * P, a * UW:(a + 1) * UW].rearrange("p (k f) -> p k f", k=1))
                elif kind == "win":
                    load(n, w_in[0].rearrange("(h k p) n -> h p k n", h=2, p=P)[b][:, :, a * 512:(a + 1) * 512])
                else:
                    load(n, w_out[0].rearrange("(h k p) n -> h p k n", h=4, p=P)[a])

            def stream(p):
                first = N_EXPERTS * p * UPE
                for u in range(2 * UPE):
                    if p == 0:
                        wait_reader(BASE + u - RING)
                    else:
                        sp.wait_ge(split_used, first + u + 1 - RING)
                    if p == 0 and u == SPARE:
                        load(BASE + u, unit_source(2 + u // UPE, u % UPE))
                    else:
                        load(BASE + u, unit_source(u // UPE, u % UPE))
                if p == 0:
                    sp.wait_ge(h3_ready, TT)
                    sp.dma_start(Hn[:].rearrange("p t (two f) -> p (t two) f", two=2), unit_source(SPARE // UPE, SPARE % UPE)).then_inc(spare_in, 16)
                    for u in range(2 * UPE):
                        if u != SPARE:
                            sp.wait_ge(split_used, u + 1)
                            load(BASE + u, unit_source(2 + u // UPE, u % UPE))
                with sp.Fori(2 if p == 0 else 1, N_EXPERTS // 2) as i:
                    for u in range(2 * UPE):
                        sp.wait_ge(split_used, i * (2 * UPE) + (first + u + 1 - RING))
                        load(BASE + u, unit_source(i * 2 + u // UPE, u % UPE))

            stream(0)
            sp.wait_ge(placed, 1)
            most = sp.value_load(maxcnt[0:1, 0:1], min_val=0, max_val=SEQ)
            for p in range(1, PASSES):
                with sp.If(most > SLOTS * p):
                    stream(p)
            out_v = out[0].rearrange("(t p) d -> p t d", p=P)
            for part in range(2 * TT):
                t, cols = part // 2, slice(part % 2 * 512, part % 2 * 512 + 512)
                sp.wait_ge(final_row, part + 1)
                sp.dma_start(out_v[:, t, cols], Hn[:, t, cols]).then_inc(stored, 16)
            sp.wait_ge(stored, 16 * 2 * TT)

        @block.gpsimd
        def _(pool):
            nc.gpsimd.memset(ones[:], 1.0).then_inc(pool_step, 1)
            nc.gpsimd.memset(epsb[:], EPS).then_inc(consts, 1)
            pool.wait_ge(pool_step, 1)
            nc.gpsimd.affine_select(out=ident[:], in_=ones[:], compare_op=ALU.is_equal, fill=0.0, base=0,
                                    pattern=[[-1, P]], channel_multiplier=1).then_inc(consts, 1)
            nc.gpsimd.affine_select(out=flip[:], in_=ones[:], compare_op=ALU.is_equal, fill=0.0, base=1 - P,
                                    pattern=[[1, P]], channel_multiplier=1).then_inc(consts, 1)
            nc.gpsimd.affine_select(out=before[:], in_=ones[:], compare_op=ALU.is_gt, fill=0.0, base=0,
                                    pattern=[[1, P]], channel_multiplier=-1).then_inc(consts, 1)
            nc.gpsimd.iota(slot_no[:], pattern=[[0, 2], [1, SLOTS]], base=0, channel_multiplier=0,
                           allow_small_or_imprecise_dtypes=True).then_inc(consts, 1)
            nc.gpsimd.iota(num32[:], pattern=[[0, TT], [1, N_EXPERTS]], base=-64, channel_multiplier=0,
                           allow_small_or_imprecise_dtypes=True).then_inc(consts, 1)
            nc.gpsimd.memset(MOD[:, 2 * D:], 0.0).then_inc(rest_zero, 1)
            nc.gpsimd.memset(line[:], NEG).then_inc(pool_step, 1)
            pool.wait_ge(pool_step, 2)
            pool.wait_ge(tab_in, 16)
            spread = buckets()
            for lo, hi, b in spread:
                nc.gpsimd.tensor_scalar(line[:, 255 - hi:256 - lo], ones[0:N_BIAS, 0:1].to_broadcast([N_BIAS, hi - lo + 1]),
                                        tabT[:, b:b + 1], None, ALU.mult).then_inc(table_set, 1)
            pool.wait_ge(table_set, len(spread))
            pool.dma_start(line_dram, line[:]).then_inc(line_out, 16)
            pool.wait_ge(line_out, 16)
            pool.wait_ge(unit_in[DC - 2], 16)
            pool.dma_start(toe[:], bass.AP(line_dram.tensor, 0, [[1, P], [3 * P, N_BIAS], [1, SEQ]])).then_inc(toe_in, 16)

            pool.wait_ge(consts, 2)
            nc.gpsimd.tensor_copy(ident16[:], ident[:]).then_inc(consts, 1)
            nc.gpsimd.tensor_tensor(stack2[:], ident[:, 0:SLOTS], ident[:, SLOTS:P], ALU.add).then_inc(consts, 1)
            pool.wait_ge(inv_rms, 1)
            n = N_DIFF * TT
            nc.gpsimd.tensor_tensor(diag, ident[:].rearrange("p (o q) -> p o q", o=1).to_broadcast([P, n, P]),
                                    st[:, 56:56 + n].rearrange("p (n o) -> p n o", o=1).to_broadcast([P, n, P]),
                                    ALU.mult).then_inc(diag_ready, 1)

            pool.wait_ge(gain_in, 48)
            pool.wait_ge(mod_row, 2)
            nc.gpsimd.tensor_tensor(MOD[:, 2 * D:3 * D], MOD[:, 2 * D:3 * D], gain[:, 1, :], ALU.mult).then_inc(gained, 1)
            pool.wait_ge(mod_row, 4)
            nc.gpsimd.tensor_tensor(MOD[:, 4 * D:5 * D], MOD[:, 4 * D:5 * D], gain[:, 2, :], ALU.mult).then_inc(gained, 1)
            pool.wait_ge(mod_row, 5)
            nc.gpsimd.tensor_tensor(G2[:], G2[:], MOD[:, 5 * D:], ALU.mult).then_inc(gained, 1)

            def column(e, buf):
                nc.gpsimd.tensor_copy(cur[:, buf, :, :], PG[:, bass.ds(e, 1), :, :].rearrange("p e a t -> p (e a) t")).then_inc(cur_ready, 1)

            def prepare(e, buf, m, n):
                pool.wait_ge(cur_ready, m)
                if not isinstance(n, int) or n:
                    pool.wait_ge(onehot_ready, n * (2 * TT))
                column(e + 1, 1 - buf)
                for t in range(TT):
                    nc.gpsimd.tensor_scalar(OH[:, buf, t, :], slot_no[:], cur[:, buf, 0, t:t + 1], None,
                                            ALU.is_equal).then_inc(onehot_ready, 1)
                for t in range(TT):
                    nc.gpsimd.tensor_scalar(OG[:, buf, t, :], slot_no[:], cur[:, buf, 0, t:t + 1],
                                            cur[:, buf, 1, t:t + 1], ALU.is_equal, ALU.mult).then_inc(onehot_ready, 1)

            def one_pass(p):
                at = (N_EXPERTS + 1) * p
                if p == 0:
                    pool.wait_ge(placed, 1)
                else:
                    pool.wait_ge(pass_shift, p)
                    pool.wait_ge(prep_mm, N_EXPERTS * p)
                    pool.wait_ge(cur_ready, at)
                column(0, 0)
                prepare(0, 0, at + 1, N_EXPERTS * p)
                prepare(1, 1, at + 2, N_EXPERTS * p + 1)
                with pool.Fori(1, N_EXPERTS // 2) as i:
                    for odd in (0, 1):
                        n = experts_before(i, odd, p)
                        pool.wait_ge(prep_mm, n - 1)
                        prepare(i * 2 + odd, odd, i * 2 + (odd + 1 + at), n)

            all_passes(pool, one_pass)

        @block.scalar
        def _(act):
            def broadcast(row, n):
                return bass.AP(row.tensor, row.offset, [[0, P], [1, n]])

            with nc.allow_non_contiguous_dma(reason="small columns"):
                act.dma_start(cT[:], c.rearrange("b (k p) -> p (b k)", p=P)).then_inc(c_in, 16)
                act.dma_start(tabT[:], rel_bias.rearrange("b h -> h b")).then_inc(tab_in, 16)
                act.wait_ge(mod_zero, 1)
                act.dma_start(MOD[0:1, 0:2 * D], b_ada[:, 0:2 * D]).then_inc(ada_b_in, 16)
                act.dma_start(X[:], x[0].rearrange("(t p) d -> p t d", p=P)).then_inc(x_in, 16)
                act.dma_start(gain[:, 0, :], broadcast(pre_mix_gain, D)).then_inc(pre_gain_in, 16)
                act.wait_ge(c_in, 16)
                nc.scalar.activation(cS[:], cT[:], ACT.Silu).then_inc(c_silu, 1)
                act.wait_ge(rest_zero, 1)
                act.dma_start(MOD[0:1, 2 * D:], b_ada[:, 2 * D:]).then_inc(ada_b_rest, 16)

            def root_mean(n, source, squares):
                nc.scalar.activation(squares, source, ACT.Square, accum_out=st[:, n:n + 1]).then_inc(stat_sq, 1)
                act.wait_ge(stat_sq, n + 1)
                nc.scalar.activation(st[:, n:n + 1], st[:, n:n + 1], ACT.Sqrt, bias=epsb[:], scale=1.0 / D).then_inc(stat_std, 1)

            act.wait_ge(x_in, 16)
            act.wait_ge(consts, 1)
            for t in range(TT):
                root_mean(t, X[:, t, :], Hn[:, t, :])
            act.wait_ge(ada_mm, DC // 2)
            nc.scalar.copy(MOD[:, 0:D], PS[:, 0:2, :].rearrange("p b f -> p (b f)")).then_inc(mod_row, 1)

            def bias_matrix(b):
                act.wait_ge(toe_mm, b + 1)
                nc.scalar.copy(toe[:, 2 * b:2 * b + 2, :], PS[:, 4 + b % 4, :].rearrange("p (h j) -> p h j", h=2)).then_inc(toe_ready, 1)

            for b in range(4):
                bias_matrix(b)
            for g in range(4):
                act.wait_ge(hT_mm, g + 1)
                nc.scalar.copy(hT[:, 4 * (g % 2):4 * (g % 2) + 4, (g // 2) * P:(g // 2 + 1) * P],
                               PS[:, 4 + g, :].rearrange("p (k t) -> p k t", k=4)).then_inc(hT_ready, 1)

            def projection(half):
                b, h = half // 2, half % 2
                act.wait_ge(win_used, half + 1)
                bank = PS[:, projection_bank(b, h), :]
                if b in (2, 5):
                    nc.scalar.copy(Hn[:, h, (b // 3) * 512:(b // 3) * 512 + 512], bank).then_inc(proj_ready, 1)
                else:
                    chunk = {0: 0, 1: 4, 3: 8, 4: 12}[b] + 2 * h
                    nc.scalar.mul(qkT[:, chunk:chunk + 2, :], bank.rearrange("p (s t) -> p s t", t=SEQ),
                                  HEAD ** -0.5 if b in (0, 3) else 1.0).then_inc(proj_ready, 1)

            def exps(g):
                act.wait_ge(negmax, 2 * (g + 1))
                for m in range(2):
                    for t, cols in ((0, slice(0, P)), (1, slice(P, 3 * P))):
                        col = 16 + 8 * (g % 2) + 2 * t + m
                        nc.scalar.activation(S[:, g % 2, m, cols], S[:, g % 2, m, cols], ACT.Exp,
                                             bias=st[:, col:col + 1],
                                             accum_out=st[:, col + 4:col + 5]).then_inc(exp_ready, 1)

            def transposed(g):
                act.wait_ge(pt_mm, g + 1)
                if g:
                    act.wait_ge(pv_mm, g)
                maps = 1 if g < N_DIFF else 2
                nc.scalar.copy(PT[:, 0:maps, :], PS[:, 4:4 + maps, 0:3 * P]).then_inc(pt_ready, 1)

            def outputs(g):
                act.wait_ge(pv_mm, g + 1)
                y = PS[:, value_bank(g), 0:SEQ]
                nc.scalar.copy(qkT[:, output_chunk(g), :], y).then_inc(y_ready, 1)
                if g < N_DIFF:
                    nc.scalar.activation(sq[:, g * SEQ:(g + 1) * SEQ], y, ACT.Square).then_inc(y_ready, 1)

            with nc.allow_non_contiguous_dma(reason="small columns"):
                for n, row in enumerate((lambda_q1, lambda_q2, lambda_k1, lambda_k2)):
                    act.dma_start(lams[:, n, :], broadcast(row, HEAD)).then_inc(lam_in, 16)
                act.dma_start(hgain[:], diff_head_gain.rearrange("l d -> d l")).then_inc(hgain_in, 16)
                act.dma_start(gain[:, 1, :], broadcast(post_mix_gain, D)).then_inc(gain_in, 16)
                act.dma_start(gain[:, 2, :], broadcast(pre_ffn_gain, D)).then_inc(gain_in, 16)
                act.dma_start(G2[:], broadcast(post_ffn_gain, D)).then_inc(gain_in, 16)
                act.dma_start(wr[:, :, 0:N_GROUPS], w_group[0].rearrange("(k p) n -> p k n", p=P)).then_inc(router_in, 16)
                act.dma_start(wr[:, :, N_GROUPS:], w_expert[0].rearrange("(k p) n -> p k n", p=P)).then_inc(router_in, 16)
                act.dma_start(brow[:, 0:N_GROUPS], b_group).then_inc(router_in, 16)
                act.dma_start(brow[:, N_GROUPS:], b_expert).then_inc(router_in, 16)
            projection(0)
            projection(1)
            projection(2)
            projection(3)
            for b in (4, 5):
                bias_matrix(b)
            projection(4)
            projection(5)
            act.wait_ge(lam_sum, 1)
            nc.scalar.activation(st[:, 10:12], st[:, 8:10], ACT.Exp).then_inc(lam_exp, 1)
            exps(0)
            for j in range(6):
                projection(6 + j)
                if j < N_DIFF:
                    transposed(j)
                if 1 <= j <= N_DIFF:
                    outputs(j - 1)
                if j < N_DIFF - 1:
                    exps(j + 1)
                if j == 4:
                    exps(4)
            for g in range(N_DIFF, PAIRS):
                transposed(g)
                if g == 4:
                    exps(5)
                if g + 2 < PAIRS:
                    exps(g + 2)
                if g == 4:
                    act.wait_ge(sq_mm, 1)
                    nc.scalar.activation(st[:, 56:64], PS[:, 7, 0:N_DIFF * TT], ACT.Sqrt, bias=epsb[:],
                                         scale=1.0 / (2 * HEAD)).then_inc(rms_ready, 1)
                part = g - 2
                act.wait_ge(mod_mm, part - 1)
                into = MOD[:, part * D:(part + 1) * D]
                if part == 4:
                    nc.scalar.activation(into, PS[:, 0:2, :].rearrange("p b f -> p (b f)"), ACT.Identity,
                                         bias=ones[:, 0:1]).then_inc(mod_row, 1)
                else:
                    nc.scalar.copy(into, PS[:, 0:2, :].rearrange("p b f -> p (b f)")).then_inc(mod_row, 1)
                outputs(g)
            nc.scalar.activation(st[:, 14:15], epsb[:], ACT.Sqrt).then_inc(warm, 1)
            act.wait_ge(pv_mm, PAIRS)
            act.wait_ge(gained, 3)
            for u in range(SPLITS):
                act.wait_ge(unit_in[ring_slot(0, u)], 16 * uses_of(BASE + u))
                nc.scalar.copy(WH[:, u, :], W[ring_slot(0, u)][:]).then_inc(hi_ready, 1)

            def h2_transposed(t):
                for g in (2 * t, 2 * t + 1):
                    act.wait_ge(hT_mm, 4 + g + 1)
                    nc.scalar.copy(hT[:, 4 * (g % 2):4 * (g % 2) + 4, t * P:(t + 1) * P],
                                   PS[:, 4 + g, :].rearrange("p (k t) -> p k t", k=4)).then_inc(hT_ready, 1)

            for t in range(TT):
                act.wait_ge(out_mm, t + 1)
                root_mean(2 + 2 * t, OUT[:, t, :], sq)
                if t:
                    h2_transposed(0)
                act.wait_ge(x2_ready, t + 1)
                root_mean(3 + 2 * t, X[:, t, :], sq)
            h2_transposed(1)
            for part in range(2):
                for t in range(TT):
                    if part:
                        act.wait_ge(rest_ready, t + 1)
                    nc.scalar.copy(H3[:, part, t, :], Hn[:, t, :]).then_inc(part_ready, 1)
            act.wait_ge(group_sub, 1)
            nc.scalar.activation(rt[:, 0, :, 0:N_GROUPS], rt[:, 0, :, 0:N_GROUPS], ACT.Exp).then_inc(group_exp, 1)
            act.wait_ge(pair_sub, 1)
            nc.scalar.activation(st[:, 44:46], st[:, 44:46], ACT.Exp).then_inc(pair_exp, 1)
            nc.scalar.activation(st[:, 15:16], epsb[:], ACT.Silu).then_inc(warm, 1)
            act.wait_ge(pos_mm, 1)

            def one_pass(p):
                def split_high(i, odd, u):
                    if ahead(i, odd, u, p):
                        return
                    n = units_before(i, odd, p, u)
                    unit_arrived(act, i, odd, u, p)
                    if turn_in_pass(i, odd) or u >= SPLITS or p:
                        act.wait_ge(split_used, n + (1 - SPLITS))
                    source = Hn[:].rearrange("p t f -> p (t f)") if is_spare(i, odd, u, p) else W[ring_slot(odd, u)][:]
                    nc.scalar.copy(WH[:, (UPE * odd + u) % SPLITS, :], source).then_inc(hi_ready, 1)

                def output_high(buf, units):
                    act.wait_ge(split_used, units)
                    nc.scalar.mul(YH[:], PS[:, 2:4, :].rearrange("p b f -> p (b f)"),
                                  gcol[:, buf:buf + 1]).then_inc(yh_ready, 1)

                def tokens(n):
                    act.wait_ge(gather_mm, n + 1)
                    nc.scalar.copy(XT[:, :, 0, :], PS[:, 2, :].rearrange("p (k s) -> p k s", k=DC)).then_inc(xh_ready, 1)

                def gate_up(n):
                    act.wait_ge(split_used, n * UPE + 4)
                    nc.scalar.copy(GU[:], PS[:, 0:2, :].rearrange("p b f -> p (b f)")).then_inc(gu_read, 1)

                def silu(n):
                    act.wait_ge(gt_mm, n + 1)
                    nc.scalar.activation(SG[:], PS[:, 0, 0:FC * SLOTS], ACT.Silu).then_inc(silu_ready, 1)

                def slots(n, buf, used):
                    act.wait_ge(prep_mm, n + 1)
                    if used:
                        act.wait_ge(scat_mm, n - 1)
                    nc.scalar.copy(ST[:, buf, :], PS[:, 1, :].bitcast(bf16)[:, 0:SEQ]).then_inc(scatT_ready, 1)
                    nc.scalar.copy(gcol[:, buf:buf + 1], PS[:, 1, SEQ:SEQ + 1]).then_inc(scatT_ready, 1)

                def pair(i):
                    for odd in (0, 1):
                        n = experts_before(i, odd, p)
                        turn = turn_in_pass(i, odd)
                        if turn:
                            gate_up(n - 1)
                        split_high(i, odd, 0)
                        tokens(n)
                        if turn:
                            silu(n - 1)
                        split_high(i, odd, 1)
                        slots(n, odd, turn == 2 or p)
                        split_high(i, odd, 2)
                        if turn:
                            output_high(1 - odd, units_before(i, odd, p, 0))
                        for u in (3, 4):
                            split_high(i, odd, u)
                        if is_last(i, odd):
                            gate_up(n)
                        split_high(i, odd, 5)

                by_pairs(act, pair)
                end = N_EXPERTS * (p + 1)
                silu(end - 1)
                nc.scalar.activation(st[:, 14:15], epsb[:], ACT.Sqrt).then_inc(warm, 1)
                output_high(1, UPE * end)
                act.wait_ge(scat_mm, end)

            act.wait_ge(placed, 1)
            all_passes(act, one_pass)
            for t in range(TT):
                root_mean(6 + t, ACC[:, t, :], junk)

        @block.vector
        def _(dve):
            steps = [0]

            def link(ins):
                steps[0] += 1
                ins.then_inc(dve_step, 1)
                dve.wait_ge(dve_step, steps[0])

            def ada(n):
                _, a, k = ADA_ORDER[n]
                at = UNIT_AT[ADA_ORDER[n]]
                dve.wait_ge(unit_in[slot_of(at)], 16 * uses_of(at))
                if n:
                    dve.wait_ge(ada_used, n)
                m = MOD[:, a * UW:(a + 1) * UW]
                nc.vector.scalar_tensor_tensor(m, W[slot_of(at)][:, :], cS[:, k:k + 1], m,
                                               ALU.mult, ALU.add).then_inc(ada_used, 1)

            nc.vector.memset(MOD[:, 0:2 * D], 0.0).then_inc(mod_zero, 1)
            dve.wait_ge(c_silu, 1)
            nc.vector.tensor_copy(cSb, cS[:].rearrange("p (k two) -> p k two", two=2)[:, :, 1:2].to_broadcast([P, DC // 2, P])).then_inc(cs_ready, 1)
            dve.wait_ge(ada_b_in, 16)
            for n in range(FIRST_ADA):
                ada(n)

            def inverse(n):
                dve.wait_ge(stat_std, n + 1)
                nc.vector.reciprocal(st[:, 48 + n:49 + n], st[:, n:n + 1]).then_inc(stat_inv, 1)

            def modulate(t, scale, shift, n):
                dve.wait_ge(stat_inv, n + 1)
                link(nc.vector.scalar_tensor_tensor(Hn[:, t, :], X[:, t, :], st[:, 48 + n:49 + n], scale, ALU.mult, ALU.mult))
                nc.vector.tensor_tensor(Hn[:, t, :], Hn[:, t, :], shift, ALU.add).then_inc(h_ready, 1)

            inverse(0)
            inverse(1)
            dve.wait_ge(pre_gain_in, 16)
            dve.wait_ge(ada_mm, DC // 2)
            link(nc.vector.scalar_tensor_tensor(MOD[:, D:2 * D], PS[:, 2:4, :].rearrange("p b f -> p (b f)"), 1.0, gain[:, 0, :],
                                                ALU.add, ALU.mult))
            dve.wait_ge(mod_row, 1)
            for t in range(TT):
                modulate(t, MOD[:, D:2 * D], MOD[:, 0:D], t)

            dve.wait_ge(ada_b_rest, 16)
            for n in range(FIRST_ADA, FIRST_ADA + 9):
                ada(n)
            dve.wait_ge(lam_in, 64)
            link(nc.vector.tensor_tensor(lams[:, 0:2, :], lams[:, 0:2, :], lams[:, 2:4, :], ALU.mult))
            nc.vector.tensor_reduce(st[:, 8:10], lams[:, 0:2, :], AX.X, ALU.add).then_inc(lam_sum, 1)
            dve.wait_ge(lam_exp, 1)
            link(nc.vector.tensor_tensor(st[:, 12:13], st[:, 11:12], st[:, 10:11], ALU.subtract))
            link(nc.vector.tensor_scalar(st[:, 13:14], st[:, 12:13], -LAMBDA_INIT, None, ALU.add))
            dve.wait_ge(hgain_in, 16)
            link(nc.vector.tensor_scalar(hgain[:], hgain[:], 1.0 - LAMBDA_INIT, None, ALU.mult))
            dve.wait_ge(toe_ready, 6)

            def scores(g):
                if g >= 2:
                    dve.wait_ge(pt_mm, g - 1)
                dve.wait_ge(score_mm, g + 1)
                s0 = 16 + 8 * (g % 2)
                for t, cols, j in ((0, slice(0, P), slice(P, 2 * P)), (1, slice(P, 3 * P), slice(0, 2 * P))):
                    if g < N_DIFF:
                        bias = toe[:, g:g + 1, j].to_broadcast([P, 2, j.stop - j.start])
                    else:
                        h = N_DIFF + 2 * (g - N_DIFF)
                        bias = toe[:, h:h + 2, j]
                    nc.vector.tensor_tensor(S[:, g % 2, :, cols], PS[:, 2:4, cols], bias, ALU.add).then_inc(score_read, 1)
                for t, cols in ((0, slice(0, P)), (1, slice(P, 3 * P))):
                    dve.wait_ge(score_read, 2 * g + 1 + t)
                    nc.vector.tensor_reduce(st[:, s0 + 2 * t:s0 + 2 * t + 2], S[:, g % 2, :, cols], AX.X, ALU.max,
                                            negate=True).then_inc(negmax, 1)

            def probabilities(g):
                dve.wait_ge(exp_ready, 4 * (g + 1))
                s0 = 16 + 8 * (g % 2)
                inv = 32 + 4 * (g % 2)
                link(nc.vector.reciprocal(st[:, inv:inv + 4], st[:, s0 + 4:s0 + 8]))
                if g < N_DIFF:
                    for t in range(2):
                        link(nc.vector.tensor_tensor(st[:, 40 + t:41 + t], st[:, inv + 2 * t + 1:inv + 2 * t + 2], st[:, 13:14], ALU.mult))
                for t, cols in ((0, slice(0, P)), (1, slice(P, 3 * P))):
                    for m in range(2):
                        e = S[:, g % 2, m, cols]
                        r = st[:, inv + 2 * t + m:inv + 2 * t + m + 1]
                        if g < N_DIFF and m == 1:
                            r = st[:, 40 + t:41 + t]
                        ins = nc.vector.tensor_scalar(e, e, r, None, ALU.mult)
                        if g >= N_DIFF:
                            ins.then_inc(prob_ready, 1)
                        elif m == 1:
                            link(ins)
                    if g < N_DIFF:
                        nc.vector.tensor_tensor(S[:, g % 2, 0, cols], S[:, g % 2, 0, cols], S[:, g % 2, 1, cols],
                                                ALU.add).then_inc(prob_ready, 2)

            scores(0)
            ada(FIRST_ADA + 9)
            probabilities(0)
            for g in range(1, 5):
                if g == 1:
                    ada(FIRST_ADA + 10)
                scores(g)
                ada(FIRST_ADA + 10 + g)
                probabilities(g)
            scores(5)
            ada(FIRST_ADA + 15)
            scores(6)
            probabilities(5)
            dve.wait_ge(rms_ready, 1)
            nc.vector.reciprocal(st[:, 56:64], st[:, 56:64]).then_inc(inv_rms, 1)

            def scale_diff(half):
                dve.wait_ge(rms_mm, half + 1)
                yd = qkT[:, 2 * half:2 * half + 2, :].rearrange("p h t -> p (h t)")
                nc.vector.scalar_tensor_tensor(yd, yd, hgain[:], PS[:, 7, :], ALU.mult, ALU.mult).then_inc(ydiff_ready, 1)

            scores(7)
            probabilities(6)
            scale_diff(0)
            probabilities(7)
            scale_diff(1)
            for u in range(SPLITS):
                dve.wait_ge(hi_ready, u + 1)
                nc.vector.tensor_tensor(WL[ring_slot(0, u)][:], W[ring_slot(0, u)][:], WH[:, u, :].bitcast(f32),
                                        ALU.subtract).then_inc(lo_ready, 1)
            dve.wait_ge(gained, 3)
            for t in range(TT):
                n = 2 + 2 * t
                dve.wait_ge(stat_sq, n + 1)
                link(nc.vector.tensor_tensor(Hn[:, t, :], OUT[:, t, :], MOD[:, 2 * D:3 * D], ALU.mult))
                inverse(n)
                dve.wait_ge(stat_inv, n + 1)
                nc.vector.scalar_tensor_tensor(X[:, t, :], Hn[:, t, :], st[:, 48 + n:49 + n], X[:, t, :],
                                               ALU.mult, ALU.add).then_inc(x2_ready, 1)
                dve.wait_ge(x2_ready, t + 1)
                link(nc.vector.tensor_tensor(Hn[:, t, :], X[:, t, :], MOD[:, 4 * D:5 * D], ALU.mult))
                inverse(n + 1)
                dve.wait_ge(stat_inv, n + 2)
                nc.vector.scalar_tensor_tensor(Hn[:, t, :], Hn[:, t, :], st[:, 49 + n:50 + n], MOD[:, 3 * D:4 * D],
                                               ALU.mult, ALU.add).then_inc(h_ready, 1)
            nc.vector.memset(GU[:, 0:256], 0.0).then_inc(zero_ready, 1)

            for t in range(TT):
                dve.wait_ge(hT_mm, 4 + 2 * (t + 1))
                dve.wait_ge(part_ready, t + 1)
                nc.vector.tensor_tensor(Hn[:, t, :], Hn[:, t, :], H3[:, 0, t, :], ALU.subtract).then_inc(rest_ready, 1)
            R = [rt[:, k, :, :] for k in range(10)]
            L = logits[:]
            G, E = L[:, :, 0:N_GROUPS], L[:, :, N_GROUPS:]
            g4 = lambda k: rt[:, k, :, 0:N_GROUPS]

            def spread(v, n):
                return v.rearrange("p (t o) -> p t o", o=1).to_broadcast([P, TT, n])

            def first_of(vals, most, k, n):
                a, b = rt[:, k, :, 0:n], rt[:, k + 1, :, 0:n]
                link(nc.vector.tensor_tensor(a, vals, spread(most, n), ALU.is_equal))
                link(nc.vector.tensor_tensor(b, a, num32[:, :, 0:n], ALU.mult))
                link(nc.vector.tensor_reduce(st[:, 46:48], b, AX.X, ALU.min))
                link(nc.vector.tensor_tensor(a, num32[:, :, 0:n], spread(st[:, 46:48], n), ALU.is_equal))
                return a

            dve.wait_ge(logit_mm, 1)
            link(nc.vector.tensor_copy(L, PS[:, 0, 0:TT * 36].rearrange("p (t n) -> p t n", t=TT)))
            gm, gw, m1, m2, d, t1 = (st[:, a:a + 2] for a in (32, 34, 36, 38, 44, 40))
            link(nc.vector.tensor_reduce(gm, G, AX.X, ALU.max))
            nc.vector.tensor_tensor(g4(0), G, spread(gm, N_GROUPS), ALU.subtract).then_inc(group_sub, 1)
            gsel = first_of(G, gm, 1, N_GROUPS)
            link(nc.vector.tensor_scalar(g4(3), gsel, -1.0, -NEG, ALU.add, ALU.mult))
            link(nc.vector.tensor_tensor(R[4].rearrange("p t (g j) -> p t g j", g=N_GROUPS),
                                         E.rearrange("p t (g j) -> p t g j", g=N_GROUPS),
                                         g4(3).rearrange("p t (g o) -> p t g o", o=1).to_broadcast([P, TT, N_GROUPS, PER_GROUP]),
                                         ALU.add))
            link(nc.vector.tensor_reduce(m1, R[4], AX.X, ALU.max))
            o1 = first_of(R[4], m1, 5, N_EXPERTS)
            link(nc.vector.scalar_tensor_tensor(R[7], o1, 3.0 * NEG, R[4], ALU.mult, ALU.add))
            link(nc.vector.tensor_reduce(m2, R[7], AX.X, ALU.max))
            nc.vector.tensor_tensor(d, m2, m1, ALU.subtract).then_inc(pair_sub, 1)
            o2 = first_of(R[7], m2, 8, N_EXPERTS)
            dve.wait_ge(group_exp, 1)
            nc.vector.tensor_tensor(R[2], o1, o2, ALU.add).then_inc(routed, 1)
            link(nc.vector.tensor_reduce(gw, g4(0), AX.X, ALU.add))
            link(nc.vector.reciprocal(gw, gw))
            dve.wait_ge(pair_exp, 1)
            link(nc.vector.tensor_scalar(t1, d, 1.0, None, ALU.add))
            link(nc.vector.reciprocal(t1, t1))
            link(nc.vector.tensor_tensor(t1, t1, gw, ALU.mult))
            link(nc.vector.tensor_tensor(d, d, t1, ALU.mult))
            link(nc.vector.tensor_tensor(R[6], o1, spread(t1, N_EXPERTS), ALU.mult))
            link(nc.vector.tensor_tensor(R[9], o2, spread(d, N_EXPERTS), ALU.mult))
            link(nc.vector.memset(PG[:], -1.0))
            link(nc.vector.memset(PG[:, :, 1, :], 0.0))
            link(nc.vector.tensor_tensor(gates[:, :, 0:N_EXPERTS], R[6], R[9], ALU.add))
            dve.wait_ge(routed, 1)
            dve.wait_ge(pos_mm, 1)
            place = PS[:, 1, 0:TT * N_EXPERTS].rearrange("p (t n) -> p t n", t=TT)
            link(nc.vector.scalar_tensor_tensor(R[1], place, 1.0, R[2], ALU.add, ALU.mult))
            link(nc.vector.tensor_scalar(posm[:, :, 0:N_EXPERTS], R[1], -1.0, None, ALU.add))
            nc.vector.tensor_reduce(maxcnt[:], PS[0:1, 1, 64:64 + N_EXPERTS], AX.X, ALU.max).then_inc(placed, 1)
            for t in range(TT):
                dve.wait_ge(part_ready, TT + t + 1)
                nc.vector.tensor_tensor(H3[:, 2, t, :], Hn[:, t, :], H3[:, 1, t, :], ALU.subtract).then_inc(h3_ready, 1)

            def one_pass(p):
                if p:
                    dve.wait_ge(onehot_ready, 2 * TT * N_EXPERTS * p)
                    nc.vector.tensor_scalar(PG[:, :, 0, :], PG[:, :, 0, :], -float(SLOTS), None, ALU.add).then_inc(pass_shift, 1)

                def split_low(i, odd, u):
                    if ahead(i, odd, u, p):
                        return
                    n = units_before(i, odd, p, u)
                    dve.wait_ge(hi_ready, n + 1)
                    source, low = W[ring_slot(odd, u)][:], WL[ring_slot(odd, u)][:]
                    if is_spare(i, odd, u, p):
                        source, low = Hn[:].rearrange("p t f -> p (t f)"), HnL[:]
                    nc.vector.tensor_tensor(low, source,
                                            WH[:, (UPE * odd + u) % SPLITS, :].bitcast(f32), ALU.subtract).then_inc(lo_ready, 1)

                def output_low(buf, done):
                    dve.wait_ge(yh_ready, done)
                    nc.vector.scalar_tensor_tensor(YL[:], PS[:, 2:4, :].rearrange("p b f -> p (b f)"), gcol[:, buf:buf + 1],
                                                   YH[:].bitcast(f32), ALU.mult, ALU.subtract).then_inc(yl_ready, 1)

                def tokens_low(n):
                    dve.wait_ge(xh_ready, n + 1)
                    nc.vector.tensor_tensor(XT[:, :, 1, :], PS[:, 2, :].rearrange("p (k s) -> p k s", k=DC),
                                            XT[:, :, 0, :].bitcast(f32), ALU.subtract).then_inc(xt_ready, 1)

                def hidden(n):
                    whole = HID[:].rearrange("p k s -> p (k s)")
                    dve.wait_ge(silu_ready, n + 1)
                    nc.vector.tensor_tensor(HT[:, :, 0, :], SG[:].rearrange("p (k s) -> p k s", k=FC),
                                            PS[:, 0, FC * SLOTS:].rearrange("p (k s) -> p k s", k=FC), ALU.mult).then_inc(hid_step, 1)
                    nc.vector.tensor_tensor(whole, SG[:], PS[:, 0, FC * SLOTS:], ALU.mult).then_inc(hid_step, 1)
                    dve.wait_ge(hid_step, n * 2 + 2)
                    nc.vector.tensor_tensor(HT[:, :, 1, :], HID[:], HT[:, :, 0, :].bitcast(f32), ALU.subtract).then_inc(hid_ready, 1)

                def pair(i):
                    for odd in (0, 1):
                        n = experts_before(i, odd, p)
                        turn = turn_in_pass(i, odd)
                        tokens_low(n)
                        if turn:
                            hidden(n - 1)
                        for u in (0, 1, 2):
                            split_low(i, odd, u)
                        if turn:
                            output_low(1 - odd, n)
                        for u in (3, 4):
                            split_low(i, odd, u)
                        if is_last(i, odd):
                            hidden(n)
                        split_low(i, odd, 5)

                by_pairs(dve, pair)
                output_low(1, N_EXPERTS * (p + 1))
                dve.wait_ge(scat_mm, N_EXPERTS * (p + 1))

            all_passes(dve, one_pass)
            for t in range(TT):
                dve.wait_ge(stat_sq, 7 + t)
                link(nc.vector.tensor_tensor(Hn[:, t, :], ACC[:, t, :], G2[:], ALU.mult))
                inverse(6 + t)
                dve.wait_ge(stat_inv, 7 + t)
                for half in range(2):
                    cols = slice(half * 512, half * 512 + 512)
                    nc.vector.scalar_tensor_tensor(Hn[:, t, cols], Hn[:, t, cols], st[:, 54 + t:55 + t], X[:, t, cols],
                                                   ALU.mult, ALU.add).then_inc(final_row, 1)

        @block.tensor
        def _(pe):
            def arrived(unit):
                at = UNIT_AT[unit]
                pe.wait_ge(unit_in[slot_of(at)], 16 * uses_of(at))

            pe.wait_ge(consts, 6)

            def sum_rows(parts, first_bank):
                for b, part in enumerate(parts):
                    last = nc.tensor.matmul(PS[:, first_bank + b, :], ones[:], part, start=True, stop=True)
                last.then_inc(mod_mm, 1)

            def mod_parts(a):
                return [MOD[:, a * D + 512 * b:a * D + 512 * b + 512] for b in range(2)]

            pe.wait_ge(cs_ready, 1)
            for i in range(DC // 2):
                if i == DC // 2 - 1:
                    pe.wait_ge(ada_used, FIRST_ADA)
                    for b, part in enumerate(mod_parts(0) + mod_parts(1)):
                        nc.tensor.matmul(PS[:, b, :], ones[:], part, start=False, stop=False)
                arrived(("ada", 0, 2 * i + 1))
                for b in range(4):
                    last = nc.tensor.matmul(PS[:, b, :], cSb[:, i, :], W[slot_of(UNIT_AT["ada", 0, 2 * i + 1])][:, b * 512:(b + 1) * 512],
                                            start=(i == 0), stop=(i == DC // 2 - 1))
                last.then_inc(ada_mm, 1)

            def transpose_h(t, before_h, bank):
                pe.wait_ge(h_ready, before_h + t + 1)
                for half in range(2):
                    for k in range(4):
                        last = nc.tensor.transpose(PS[:, bank + 2 * t + half, k * P:(k + 1) * P],
                                                   Hn[:, t, (4 * half + k) * P:(4 * half + k + 1) * P], ident[:])
                    last.then_inc(hT_mm, 1)

            def flip_bias(b):
                if b == 0:
                    pe.wait_ge(toe_in, 16)
                nc.tensor.matmul(PS[:, 4 + b % 4, :], flip[:], toe[:, 2 * b:2 * b + 2, :].rearrange("p h j -> p (h j)"),
                                 start=True, stop=True).then_inc(toe_mm, 1)

            for b in range(4):
                flip_bias(b)
            for t in range(TT):
                pe.wait_ge(toe_ready, 2 * (t + 1))
                transpose_h(t, 0, 4)
            pe.wait_ge(hT_ready, 4)
            def projection(b, half):
                arrived(("win", b, 0))
                arrived(("win", b, 1))
                if b >= 2:
                    pe.wait_ge(proj_ready, 2 * (b - (2 if b == 2 else 1)) + half + 1)
                w = [W[slot_of(UNIT_AT["win", b, k // 4])][:, (k % 4) * 512:(k % 4 + 1) * 512] for k in range(DC)]
                bank = projection_bank(b, half)
                if b in (2, 5):
                    for k in range(DC):
                        last = nc.tensor.matmul(PS[:, bank, :], hT[:, k, half * P:(half + 1) * P], w[k],
                                                start=(k == 0), stop=(k == DC - 1))
                else:
                    for s in range(2):
                        c0 = (2 * half + s) * P
                        for k in range(DC):
                            last = nc.tensor.matmul(PS[:, bank, s * SEQ:(s + 1) * SEQ], w[k][:, c0:c0 + P], hT[:, k, :],
                                                    start=(k == 0), stop=(k == DC - 1))
                last.then_inc(win_used, 1)

            def score(g):
                if g < N_DIFF:
                    q, k = g, 4 + g
                else:
                    q, k = 8 + g - N_DIFF, 12 + g - N_DIFF
                pe.wait_ge(proj_ready, 4 if g < N_DIFF else 10)
                if g:
                    pe.wait_ge(score_read, 2 * g)
                for t in range(TT):
                    for m in range(2):
                        half = slice(64 * m, 64 * m + 64)
                        last = nc.tensor.matmul(PS[:, 2 + m, (0 if t == 0 else P):(P if t == 0 else 3 * P)],
                                                qkT[half, q, t * P:(t + 1) * P], qkT[half, k, 0:(t + 1) * P],
                                                start=True, stop=True)
                last.then_inc(score_mm, 1)

            def transpose_probabilities(g):
                pe.wait_ge(prob_ready, 4 * (g + 1))
                if g:
                    pe.wait_ge(pt_ready, g)
                for m in range(1 if g < N_DIFF else 2):
                    for n in range(3):
                        last = nc.tensor.transpose(PS[:, 4 + m, n * P:(n + 1) * P], S[:, g % 2, m, n * P:(n + 1) * P], ident[:])
                last.then_inc(pt_mm, 1)

            def weigh_values(g):
                pe.wait_ge(pt_ready, g + 1)
                if 2 <= g < N_DIFF:
                    pe.wait_ge(y_ready, 2 * (g - 1))
                if g == N_DIFF:
                    pe.wait_ge(proj_ready, 12)
                if g > N_DIFF:
                    pe.wait_ge(y_ready, N_DIFF + g)
                bank = value_bank(g)
                if g < N_DIFF:
                    jobs = [(0, slice(0, P), Hn[:, 0, g * P:(g + 1) * P], Hn[:, 1, g * P:(g + 1) * P])]
                else:
                    jobs = []
                    for m in range(2):
                        c0 = 512 + (2 * (g - N_DIFF) + m) * HEAD
                        jobs.append((m, slice(64 * m, 64 * m + 64), Hn[:, 0, c0:c0 + HEAD], Hn[:, 1, c0:c0 + HEAD]))
                for m, rows, v0, v1 in jobs:
                    nc.tensor.matmul(PS[rows, bank, 0:SEQ], v0, PT[:, m, 0:SEQ], start=True, stop=False)
                    last = nc.tensor.matmul(PS[rows, bank, P:SEQ], v1, PT[:, m, SEQ:3 * P], start=False, stop=True)
                last.then_inc(pv_mm, 1)

            def sum_part(a):
                pe.wait_ge(ada_used, FIRST_ADA + DC * (a // 2))
                if a == 2:
                    pe.wait_ge(proj_ready, 12)
                else:
                    pe.wait_ge(mod_row, a - 1)
                sum_rows(mod_parts(a), 0)

            def spread_inverse(half):
                if half == 0:
                    pe.wait_ge(diag_ready, 1)
                else:
                    pe.wait_ge(ydiff_ready, half)
                nc.tensor.matmul(PS[:, 7, :], ones[:], diag[:, 4 * half:4 * half + 4, :].rearrange("p n q -> p (n q)"),
                                 start=True, stop=True).then_inc(rms_mm, 1)

            projection(0, 0)
            projection(0, 1)
            projection(1, 0)
            projection(1, 1)
            for b in (4, 5):
                flip_bias(b)
            projection(2, 0)
            projection(2, 1)
            score(0)
            for j in range(6):
                projection(3 + j // 2, j % 2)
                if j < N_DIFF - 1:
                    score(j + 1)
                if j == 4:
                    score(4)
                if j < N_DIFF:
                    transpose_probabilities(j)
                if 1 <= j <= N_DIFF:
                    weigh_values(j - 1)
            score(5)
            transpose_probabilities(4)
            pe.wait_ge(y_ready, 2 * N_DIFF)
            for n in range(N_DIFF * TT):
                last = nc.tensor.matmul(PS[:, 7, n:n + 1], sq[:, n * P:(n + 1) * P], ones[:, 0:1], start=True, stop=True)
            last.then_inc(sq_mm, 1)
            score(6)
            sum_part(2)
            weigh_values(4)
            transpose_probabilities(5)
            score(7)
            sum_part(3)
            spread_inverse(0)
            weigh_values(5)
            transpose_probabilities(6)
            sum_part(4)
            spread_inverse(1)
            weigh_values(6)
            transpose_probabilities(7)
            sum_part(5)

            def project_out(t, rows, begin, end):
                for k in rows:
                    arrived(("wout", k // 2, 0))
                    for half in range(2):
                        wo = W[slot_of(UNIT_AT["wout", k // 2, 0])][:, (k % 2) * D + half * 512:(k % 2) * D + half * 512 + 512]
                        last = nc.tensor.matmul(PS[:, 2 * t + half, :], qkT[:, output_chunk(k), t * P:(t + 1) * P], wo,
                                                start=(begin and k == rows[0]), stop=(end and k == rows[-1]))
                if end:
                    last.then_inc(out_mm, 1)

            pe.wait_ge(ydiff_ready, 2)
            pe.wait_ge(score_read, 2 * PAIRS)
            project_out(1, [0, 1, 2, 3], True, False)
            weigh_values(7)
            pe.wait_ge(mod_row, 5)
            project_out(0, [0, 1, 2, 3], True, False)
            pe.wait_ge(y_ready, N_DIFF + PAIRS)
            project_out(0, [4, 5, 6, 7], False, True)
            project_out(1, [4, 5, 6, 7], False, True)
            pe.wait_ge(router_in, 64)
            for t in range(TT):
                transpose_h(t, 2, 4)
                pe.wait_ge(hT_ready, 4 + 2 * (t + 1))
                lg = PS[:, 0, t * 36:(t + 1) * 36]
                for k in range(DC):
                    nc.tensor.matmul(lg, hT[:, k, t * P:(t + 1) * P], wr[:, k, :], start=(k == 0), stop=False)
                last = nc.tensor.matmul(lg, ones[0:1, :], brow[0:1, :], start=False, stop=True)
            last.then_inc(logit_mm, 1)
            pe.wait_ge(routed, 1)
            m0, m1 = rt[:, 2, 0, :], rt[:, 2, 1, :]
            E = N_EXPERTS
            nc.tensor.matmul(PS[:, 1, 0:E], before[:], m0, start=True, stop=True)
            nc.tensor.matmul(PS[:, 1, E:2 * E], ones[:], m0, start=True, stop=False)
            nc.tensor.matmul(PS[:, 1, E:2 * E], before[:], m1, start=False, stop=True)
            nc.tensor.matmul(PS[:, 1, 2 * E:3 * E], ones[:], m0, start=True, stop=False)
            nc.tensor.matmul(PS[:, 1, 2 * E:3 * E], ones[:], m1, start=False, stop=True).then_inc(pos_mm, 1)
            pe.wait_ge(zero_ready, 1)
            for b in range(4):
                nc.tensor.matmul(PS[:, 4 + b, :], ident16[:], GU[:, 0:256].bitcast(bf16), start=True, stop=True)
            pe.wait_ge(placed, 1)

            pe.wait_ge(h3_ready, TT)
            def one_pass(p):
                def gather(n, buf, turn):
                    pe.wait_ge(onehot_ready, n * (2 * TT) + TT)
                    if turn == 2 or p:
                        pe.wait_ge(yl_ready, n - 1)
                    for k in range(DC):
                        for t in range(TT):
                            for part in range(3):
                                last = nc.tensor.matmul(PS[:, 2, k * SLOTS:(k + 1) * SLOTS], H3[:, part, t, k * P:(k + 1) * P],
                                                        OH[:, buf, t, 0:SLOTS], start=(t == 0 and part == 0),
                                                        stop=(t == TT - 1 and part == 2))
                    last.then_inc(gather_mm, 1)

                def transpose_gate_up(n):
                    pe.wait_ge(gu_read, n + 1)
                    for q in range(2 * FC):
                        last = nc.tensor.matmul(PS[:, 0, q * SLOTS:(q + 1) * SLOTS], GU[:, q * P:(q + 1) * P], stack2[:],
                                                start=True, stop=True)
                    last.then_inc(gt_mm, 1)

                def prepare(n, buf):
                    pe.wait_ge(onehot_ready, (n + 1) * (2 * TT))
                    for t in range(TT):
                        nc.tensor.transpose(PS[:, 1, :].bitcast(bf16)[:, t * P:(t + 1) * P], OH[:, buf, t, :], ident16[:])
                    for t in range(TT):
                        last = nc.tensor.matmul(PS[:, 1, SEQ:SEQ + 1], OG[:, buf, t, :], ones[:, 0:1],
                                                start=(t == 0), stop=(t == TT - 1))
                    last.then_inc(prep_mm, 1)

                def scatter(n, buf):
                    for y, ready in ((YH, yh_ready), (YL, yl_ready)):
                        pe.wait_ge(ready, n + 1)
                        for t in range(TT):
                            for half in range(2):
                                last = nc.tensor.matmul(PS[:, 4 + 2 * t + half, :], ST[:, buf, t * P:(t + 1) * P],
                                                        y[:, half * 512:half * 512 + 512],
                                                        start=False, stop=True, skip_group_check=True)
                    last.then_inc(scat_mm, 1)

                def unit(n, at, spare, outs):
                    for high in (True, False):
                        pe.wait_ge(hi_ready if high else lo_ready, n + 1)
                        w = WH[:, at % SPLITS, :] if high else (HnL if spare else WL[ring_slot(0, at)])[:]
                        for q in range(4):
                            bank, lhsT, begin, end = outs(q, high)
                            last = nc.tensor.matmul(PS[:, bank, :], lhsT, w[:, q * 512:(q + 1) * 512],
                                                    start=begin, stop=end)
                    last.then_inc(split_used, 1)

                def gate_up(n, i, odd):
                    pe.wait_ge(xt_ready, n + 1)
                    pe.wait_ge(scatT_ready, n * 2 + 2)
                    for u in range(4):
                        def into(q, high):
                            k = 4 * (u % 2) + q
                            return (u // 2, XT[:, k, :, :].rearrange("p a s -> p (a s)"),
                                    k == 0 and high, k == DC - 1 and not high)
                        unit(n * UPE + u, UPE * odd + u, is_spare(i, odd, u, p), into)

                def down(n, odd):
                    pe.wait_ge(hid_ready, n + 1)
                    for u in (4, 5):
                        def into(q, high):
                            k = 2 * (u - 4) + q // 2
                            return (2 + q % 2, HT[:, k, :, :].rearrange("p a s -> p (a s)"),
                                    k == 0 and high, k == FC - 1 and not high)
                        unit(n * UPE + u, UPE * odd + u, False, into)

                def pair(i):
                    for odd in (0, 1):
                        n = experts_before(i, odd, p)
                        turn = turn_in_pass(i, odd)
                        gather(n, odd, turn)
                        if turn:
                            transpose_gate_up(n - 1)
                        prepare(n, odd)
                        if turn == 2:
                            scatter(n - 2, odd)
                        if turn:
                            pe.wait_ge(xt_ready, n + 1)
                            down(n - 1, 1 - odd)
                        gate_up(n, i, odd)

                by_pairs(pe, pair)
                end = N_EXPERTS * (p + 1)
                transpose_gate_up(end - 1)
                scatter(end - 2, 0)
                down(end - 1, 1)
                scatter(end - 1, 1)

            all_passes(pe, one_pass)


_INS = ["x", "c", "w_ada", "b_ada", "pre_mix_gain", "post_mix_gain", "pre_ffn_gain", "post_ffn_gain", "w_in",
        "lambda_q1", "lambda_k1", "lambda_q2", "lambda_k2", "diff_head_gain", "w_out", "rel_bias",
        "w_group", "b_group", "w_expert", "b_expert", "w_gate", "w_up", "w_down"]
_OUT = ((1, 256, 1024), "float32")


def kernel(**inputs):
    import numpy as _np
    import concourse.bacc as _bacc
    from concourse import mybir as _mybir
    from concourse.bass_utils import run_bass_kernel_spmd as _run

    nc = _bacc.Bacc("TRN2", target_bir_lowering=False, num_devices=1)
    arrays, args = {}, []
    for name in _INS:
        a = _np.ascontiguousarray(inputs[name])
        arrays[f"in_{name}_dram"] = a
        args.append(nc.dram_tensor(f"in_{name}_dram", a.shape, _mybir.dt.from_np(a.dtype), kind="ExternalInput").ap())
    args.append(nc.dram_tensor("out_0_dram", _OUT[0], _mybir.dt.from_np(_np.dtype(_OUT[1])), kind="ExternalOutput").ap())
    build(nc, *args)
    r = _run(nc, [arrays], core_ids=[0])
    return r.results[0]["out_0_dram"]
```
